# Optimizing a Trainium2 kernel written in Bass

```python
import math
import jax, jax.numpy as jnp
from jax import lax
import numpy as np

D_MODEL = 1024
BATCH = 1
SEQ = 256
DEPTH = 2

HEAD_DIM = 64
N_HEADS = D_MODEL // HEAD_DIM
N_HEADS_DIL = (3 * N_HEADS) // 4
N_HEADS_FOX = N_HEADS - N_HEADS_DIL
D_DIL = N_HEADS_DIL * HEAD_DIM
D_FOX = N_HEADS_FOX * HEAD_DIM
D_MIX = D_DIL + D_FOX
D_PROJ = 3 * D_DIL + 3 * D_FOX + N_HEADS_FOX
DILATED_PATTERNS = ((128, 1), (512, 4), (2048, 16))
BLOCK = 128
ROPE_THETA = 10000.0
N_EXPERTS = 16
N_GROUPS = 4
EXPERTS_PER_GROUP = N_EXPERTS // N_GROUPS
TOP_K = 2
D_FF_EXPERT = D_MODEL
DEEPNORM_ALPHA = (2.0 * DEPTH) ** 0.25
DEEPNORM_BETA = (8.0 * DEPTH) ** -0.25
LN_EPS = 1e-5
RMS_EPS = 1e-6

kernel_name = 'hymba_longnet_fox_grouped_moe_deepnorm'

def layer_norm(x, g, b):
    xf = x.astype(jnp.float32)
    mu = jnp.mean(xf, axis=-1, keepdims=True)
    var = jnp.mean(jnp.square(xf - mu), axis=-1, keepdims=True)
    return ((xf - mu) * lax.rsqrt(var + LN_EPS) * g + b).astype(x.dtype)

def rms_norm(x, g):
    xf = x.astype(jnp.float32)
    ms = jnp.mean(jnp.square(xf), axis=-1, keepdims=True)
    return (xf * lax.rsqrt(ms + RMS_EPS) * g).astype(x.dtype)

def rope(t, pos):
    half = HEAD_DIM // 2
    inv = ROPE_THETA ** (-jnp.arange(half, dtype=jnp.float32) / half)
    ang = pos[:, None] * inv[None, :]
    cos, sin = jnp.cos(ang), jnp.sin(ang)
    t1 = t[..., :half].astype(jnp.float32)
    t2 = t[..., half:].astype(jnp.float32)
    return jnp.concatenate([t1 * cos - t2 * sin, t2 * cos + t1 * sin], axis=-1).astype(t.dtype)

def dilated_branch(q, k, v, window, dil):
    B, H, S, hd = q.shape
    L = S // dil
    steps = window // dil
    nb = -(-L // BLOCK)
    Lp = nb * BLOCK

    def fold(t):
        t = t.reshape(B, H, L, dil, hd).transpose(0, 1, 3, 2, 4)
        t = jnp.pad(t, ((0, 0), (0, 0), (0, 0), (0, Lp - L), (0, 0)))
        return t.reshape(B, H, dil, nb, BLOCK, hd)

    def with_prev(t):
        prev = jnp.pad(t[:, :, :, :-1], ((0, 0), (0, 0), (0, 0), (1, 0), (0, 0), (0, 0)))
        return jnp.concatenate([prev, t], axis=4)

    qb = fold(q)
    kw = with_prev(fold(k))
    vw = with_prev(fold(v))
    s = jnp.einsum('bhrnqd,bhrnkd->bhrnqk', qb, kw).astype(jnp.float32) * (hd ** -0.5)
    qi = jnp.arange(BLOCK)[:, None]
    ki = jnp.arange(2 * BLOCK)[None, :]
    delta = BLOCK + qi - ki
    kidx = jnp.arange(nb)[:, None, None] * BLOCK - BLOCK + ki
    valid = (delta >= 0) & (delta <= steps) & (kidx >= 0)
    s = jnp.where(valid, s, -jnp.inf)
    m = jnp.max(s, axis=-1)
    p = jnp.exp(s - m[..., None])
    l = jnp.sum(p, axis=-1)
    o = jnp.einsum('bhrnqk,bhrnkd->bhrnqd', p.astype(v.dtype), vw).astype(jnp.float32) / l[..., None]

    def unfold(t):
        t = t.reshape((B, H, dil, Lp) + t.shape[5:])[:, :, :, :L]
        t = jnp.swapaxes(t, 2, 3)
        return t.reshape((B, H, S) + t.shape[4:])

    return unfold(o), unfold(m), unfold(l)

def dilated_attention(q, k, v):
    res = [dilated_branch(q, k, v, w, r) for (w, r) in DILATED_PATTERNS]
    o_all = jnp.stack([r_[0] for r_ in res])
    m_all = jnp.stack([r_[1] for r_ in res])
    l_all = jnp.stack([r_[2] for r_ in res])
    wts = l_all * jnp.exp(m_all - jnp.max(m_all, axis=0, keepdims=True))
    wts = wts / jnp.sum(wts, axis=0, keepdims=True)
    return jnp.sum(o_all * wts[..., None], axis=0).astype(q.dtype)

def forgetting_attention(q, k, v, logf):
    B, H, S, hd = q.shape
    nb = S // BLOCK
    c = jnp.cumsum(logf.astype(jnp.float32), axis=-1)
    qb = q.reshape(B, H, nb, BLOCK, hd).transpose(2, 0, 1, 3, 4)
    cq = c.reshape(B, H, nb, BLOCK).transpose(2, 0, 1, 3)
    kpos = jnp.arange(S)

    def block(args):
        q_i, c_i, i = args
        s = jnp.einsum('bhqd,bhkd->bhqk', q_i, k).astype(jnp.float32) * (hd ** -0.5)
        s = s + c_i[..., :, None] - c[:, :, None, :]
        qpos = i * BLOCK + jnp.arange(BLOCK)
        s = jnp.where(kpos[None, :] <= qpos[:, None], s, -jnp.inf)
        p = jax.nn.softmax(s, axis=-1)
        return jnp.einsum('bhqk,bhkd->bhqd', p.astype(v.dtype), v)

    o = lax.map(block, (qb, cq, jnp.arange(nb)))
    return o.transpose(1, 2, 0, 3, 4).reshape(B, H, S, hd)

def hybrid_mixer(h, w_in, b_forget, g_dil, g_fox, w_out):
    B, S, _ = h.shape
    z = h @ w_in
    cuts = np.cumsum([D_DIL, D_DIL, D_DIL, D_FOX, D_FOX, D_FOX]).tolist()
    qa, ka, va, qf, kf, vf, zf = jnp.split(z, cuts, axis=-1)

    def heads(t, n):
        return t.reshape(B, S, n, HEAD_DIM).transpose(0, 2, 1, 3)

    def merge(t):
        return t.transpose(0, 2, 1, 3).reshape(B, S, -1)

    pos = jnp.arange(S, dtype=jnp.float32)
    o_dil = dilated_attention(rope(heads(qa, N_HEADS_DIL), pos),
                              rope(heads(ka, N_HEADS_DIL), pos),
                              heads(va, N_HEADS_DIL))
    logf = jax.nn.log_sigmoid((zf + b_forget).astype(jnp.float32)).transpose(0, 2, 1)
    o_fox = forgetting_attention(heads(qf, N_HEADS_FOX), heads(kf, N_HEADS_FOX),
                                 heads(vf, N_HEADS_FOX), logf)
    y = jnp.concatenate([rms_norm(merge(o_dil), g_dil), rms_norm(merge(o_fox), g_fox)], axis=-1)
    return y @ w_out

def grouped_moe(h, w_router, b_router, w_gate, w_up, w_down):
    B, S, D = h.shape
    xt = h.reshape(-1, D)
    T = xt.shape[0]
    logits = (xt @ w_router).astype(jnp.float32) + b_router.astype(jnp.float32)
    probs = jax.nn.softmax(logits, axis=-1)
    grp = probs.reshape(T, N_GROUPS, EXPERTS_PER_GROUP)
    gscore = jnp.sum(lax.top_k(grp, TOP_K)[0], axis=-1)
    gsel = jnp.argmax(gscore, axis=-1)
    in_grp = jnp.take_along_axis(grp, gsel[:, None, None], axis=1)[:, 0]
    gv, gi = lax.top_k(in_grp, TOP_K)
    experts = gsel[:, None] * EXPERTS_PER_GROUP + gi
    gates = gv / jnp.sum(gv, axis=-1, keepdims=True)

    TK = T * TOP_K
    flat_e = experts.reshape(-1).astype(jnp.int32)
    flat_t = jnp.repeat(jnp.arange(T, dtype=jnp.int32), TOP_K)
    flat_g = gates.reshape(-1)
    order = jnp.argsort(flat_e, stable=True)
    se = flat_e[order]
    counts = jnp.bincount(flat_e, length=N_EXPERTS)
    pcounts = (counts + BLOCK - 1) // BLOCK * BLOCK
    pends = jnp.cumsum(pcounts)
    pstarts = pends - pcounts
    starts = jnp.cumsum(counts) - counts
    dest = pstarts[se] + (jnp.arange(TK) - starts[se])
    NB = -(-TK // BLOCK) + N_EXPERTS
    rows = NB * BLOCK
    row_tok = jnp.full((rows,), T, jnp.int32).at[dest].set(flat_t[order])
    row_gate = jnp.zeros((rows,), jnp.float32).at[dest].set(flat_g[order])
    blk_e = jnp.minimum(jnp.searchsorted(pends, jnp.arange(NB) * BLOCK, side='right'), N_EXPERTS - 1)
    xpad = jnp.concatenate([xt, jnp.zeros((1, D), xt.dtype)], axis=0)
    xb = xpad[row_tok].reshape(NB, BLOCK, D)

    def expert_block(args):
        xblk, e = args
        a = jax.nn.silu(xblk @ w_gate[e]) * (xblk @ w_up[e])
        return a @ w_down[e]

    yb = lax.map(expert_block, (xb, blk_e)).reshape(rows, D).astype(jnp.float32)
    out = jnp.zeros((T + 1, D), jnp.float32).at[row_tok].add(yb * row_gate[:, None])[:T]
    return out.reshape(B, S, D).astype(h.dtype)

def setup_inputs(seed: int = 0) -> dict:
    key = jax.random.key(seed)
    ks = jax.random.split(key, 16)
    f32 = jnp.float32

    def nrm(k, shape, scale):
        return jax.random.normal(k, shape, f32) * scale

    x = jax.random.normal(ks[0], (BATCH, SEQ, D_MODEL), f32)
    col_scale = jnp.concatenate([
        jnp.ones((2 * D_DIL,), f32), jnp.full((D_DIL,), DEEPNORM_BETA, f32),
        jnp.ones((2 * D_FOX,), f32), jnp.full((D_FOX,), DEEPNORM_BETA, f32),
        jnp.ones((N_HEADS_FOX,), f32)])
    w_in = nrm(ks[1], (DEPTH, D_MODEL, D_PROJ), D_MODEL ** -0.5) * col_scale
    b_forget = 3.0 + nrm(ks[2], (DEPTH, N_HEADS_FOX), 0.5)
    g_dil = 1.0 + nrm(ks[3], (DEPTH, D_DIL), 0.02)
    g_fox = 1.0 + nrm(ks[4], (DEPTH, D_FOX), 0.02)
    w_out = nrm(ks[5], (DEPTH, D_MIX, D_MODEL), D_MIX ** -0.5 * DEEPNORM_BETA)
    ln1_g = 1.0 + nrm(ks[6], (DEPTH, D_MODEL), 0.02)
    ln1_b = nrm(ks[7], (DEPTH, D_MODEL), 0.02)
    w_router = nrm(ks[8], (D_MODEL, N_EXPERTS), D_MODEL ** -0.5)
    b_router = nrm(ks[9], (N_EXPERTS,), 0.01)
    w_gate = nrm(ks[10], (DEPTH, N_EXPERTS, D_MODEL, D_FF_EXPERT), D_MODEL ** -0.5)
    w_up = nrm(ks[11], (DEPTH, N_EXPERTS, D_MODEL, D_FF_EXPERT), D_MODEL ** -0.5)
    w_down = nrm(ks[12], (DEPTH, N_EXPERTS, D_FF_EXPERT, D_MODEL), D_FF_EXPERT ** -0.5 * DEEPNORM_BETA)
    ln2_g = 1.0 + nrm(ks[13], (DEPTH, D_MODEL), 0.02)
    ln2_b = nrm(ks[14], (DEPTH, D_MODEL), 0.02)
    return {'x': x, 'w_in': w_in, 'b_forget': b_forget, 'g_dil': g_dil, 'g_fox': g_fox,
            'w_out': w_out, 'ln1_g': ln1_g, 'ln1_b': ln1_b, 'w_router': w_router,
            'b_router': b_router, 'w_gate': w_gate, 'w_up': w_up, 'w_down': w_down,
            'ln2_g': ln2_g, 'ln2_b': ln2_b}

def reference(x, w_in, b_forget, g_dil, g_fox, w_out, ln1_g, ln1_b, w_router,
              b_router, w_gate, w_up, w_down, ln2_g, ln2_b):
    h = x
    for l in range(DEPTH):
        y = hybrid_mixer(h, w_in[l], b_forget[l], g_dil[l], g_fox[l], w_out[l])
        h = layer_norm(DEEPNORM_ALPHA * h + y, ln1_g[l], ln1_b[l])
        y = grouped_moe(h, w_router, b_router, w_gate[l], w_up[l], w_down[l])
        h = layer_norm(DEEPNORM_ALPHA * h + y, ln2_g[l], ln2_b[l])
    return h


_drawn_inputs = setup_inputs


def setup_inputs(seed=0):
    import zlib

    import numpy as np

    out = dict(_drawn_inputs(seed))
    spreads = {}
    factors = {'g_fox': 3.08, 'g_dil': 3.034}
    for name, (base, spread) in spreads.items():
        noise = np.random.default_rng([zlib.crc32(name.encode()), seed]).standard_normal(out[name].shape)
        drawn = base * np.exp(spread * noise) if base else spread * noise
        out[name] = __import__('jax').numpy.asarray(drawn.astype(out[name].dtype))
    for name, factor in factors.items():
        out[name] = (out[name] * factor).astype(out[name].dtype)
    return out
```

```python
from contextlib import ExitStack

import numpy as np

import concourse.bass as bass
from concourse import mybir

ALU = mybir.AluOpType
ACT = mybir.ActivationFunctionType
AX = mybir.AxisListType
F32 = mybir.dt.float32
I32 = mybir.dt.int32

P = 128
DEPTH, SEQ, D = 2, 256, 1024
HD = 64
N_DIL, N_FOX = 12, 4
HEADS = N_DIL + N_FOX
PAIRS = HEADS // 2
D_DIL, D_FOX = N_DIL * HD, N_FOX * HD
Q_DIL, K_DIL, V_DIL = 0, D_DIL, 2 * D_DIL
Q_FOX = 3 * D_DIL
K_FOX, V_FOX = Q_FOX + D_FOX, Q_FOX + 2 * D_FOX
ZF = V_FOX + D_FOX
TB = SEQ // P
KB = D // P
CH = 512
N_CH = ZF // CH
ROPE_CH = 2 * D_DIL // CH
NEXP, NGRP, EPG = 16, 4, 4
EXTRA = 3
COLS = NEXP + EXTRA + 1
SLOTS = 12
ALPHA = (2.0 * DEPTH) ** 0.25
LN_EPS, RMS_EPS = 1e-5, 1e-6
INV_SCALE = 8.0
NEG = -1e30
SKEYS = P + SEQ

C_ID, C_AID = 0, P
C_TRI0, C_TRI1 = 2 * P, 2 * P + SEQ
C_MDIL = C_TRI1 + SEQ
C_MFOX = C_MDIL + SKEYS
C_COS = C_MFOX + SKEYS
C_IOTA = C_COS + TB * 2 * 32
C_UP = C_IOTA + P
C_LO = C_UP + 8 * 16
C_L16 = C_LO + 8 * 16
C_E = C_L16 + NEXP * NEXP
C_END = C_E + NEXP


def constants():
    t = np.zeros((P, C_END), np.float32)
    p = np.arange(P)
    t[:, C_ID:C_ID + P] = np.eye(P)
    t[:, C_AID:C_AID + P] = np.eye(P) * ALPHA
    j = np.arange(SEQ)
    t[:, C_TRI0:C_TRI0 + SEQ] = p[:, None] <= j[None]
    t[:, C_TRI1:C_TRI1 + SEQ] = p[:, None] + P <= j[None]
    for b in range(TB):
        keys = np.arange(P * (b + 1))
        delta = (p[:, None] + b * P) - keys[None]
        ok = delta >= 0
        n = (ok & (delta <= 128)) * 1.0 + (ok & (delta % 4 == 0)) + (ok & (delta % 16 == 0))
        at = b * P
        bias = np.where(n > 0, INV_SCALE * np.log(np.maximum(n, 1)), NEG)
        t[:, C_MDIL + at:C_MDIL + at + len(keys)] = bias
        t[:, C_MFOX + at:C_MFOX + at + len(keys)] = np.where(ok, 0.0, NEG)
        inv = (np.float32(10000.0) ** (-np.arange(32, dtype=np.float32) / np.float32(32))).astype(np.float32)
        ang = ((p + b * P).astype(np.float32)[:, None] * inv[None]).astype(np.float32)
        t[:, C_COS + b * 64:C_COS + b * 64 + 32] = np.cos(ang)
        t[:, C_COS + b * 64 + 32:C_COS + b * 64 + 64] = np.sin(ang)
    t[:, C_IOTA:C_IOTA + P] = np.arange(1, P + 1)
    i4 = np.arange(4)
    t[:, C_UP:C_UP + 128] = np.tile((i4[None] > i4[:, None]).astype(np.float32).ravel(), 8)
    t[:, C_LO:C_LO + 128] = np.tile((i4[None] < i4[:, None]).astype(np.float32).ravel(), 8)
    e = np.arange(NEXP)
    t[:, C_L16:C_L16 + 256] = (e[None] < e[:, None]).astype(np.float32).ravel()
    t[:, C_E:C_E + NEXP] = e
    return t


def head_cols(h):
    if h < N_DIL:
        return Q_DIL + h * HD, K_DIL + h * HD, V_DIL + h * HD
    return Q_FOX + (h - N_DIL) * HD, K_FOX + (h - N_DIL) * HD, V_FOX + (h - N_DIL) * HD


def build(nc, x, w_in, b_forget, g_dil, g_fox, w_out, ln1_g, ln1_b, w_router, b_router,
          w_gate, w_up, w_down, ln2_g, ln2_b, consts, out):
    with ExitStack() as ctx:
        def sb(name, shape, dt=F32):
            return ctx.enter_context(nc.sbuf_tensor(name, shape, dt))

        def sem(name):
            return ctx.enter_context(nc.semaphore(name))

        ring = sb("ring", [P, SLOTS, 2048])
        wout = sb("wout", [P, KB, D])
        cst = sb("cst", [P, C_END])
        h = sb("h", [P, TB, D])
        actT = sb("actT", [P, KB, SEQ])
        z = sb("z", [P, TB, ZF])
        qkT = sb("qkT", [P, 2, 4, P])
        masked = sb("masked", [P, 2, SKEYS])
        probs = sb("probs", [P, 4, SKEYS])
        probsT = sb("probsT", [P, 2, SKEYS])
        decay = sb("decay", [P, TB, N_FOX, P])
        ln_gb = sb("ln_gb", [P, 2, D])
        wf = sb("wf", [P, KB, N_FOX])
        bf = sb("bf", [P, 1, N_FOX])
        gmix = sb("gmix", [P, KB])
        wr = sb("wr", [P, KB, NEXP])
        br = sb("br", [P, 1, NEXP])
        fg = sb("fg", [P, 7, TB, N_FOX])
        row_max = sb("row_max", [P, 2, TB])
        neg_max = sb("neg_max", [P, 4, TB])
        row_sum = sb("row_sum", [P, 4, TB])
        row_inv = sb("row_inv", [P, 2, TB])
        ssq = sb("ssq", [P, TB, 2])
        rms = sb("rms", [P, 3, TB, 2])
        stats = sb("stats", [P, TB, 2, 6])
        mv = sb("mv", [P, TB, 2])
        lnt = sb("lnt", [P, 3, TB])
        rt = sb("rt", [P, 6, TB, NEXP])
        r8 = sb("r8", [P, 6, 8])
        r2 = sb("r2", [P, 5, TB])
        cmp = probs[:].rearrange("p a b -> p (a b)")[:, 0:512].rearrange("p (a b) -> p a b", a=2)
        sel = sb("sel", [P, TB, NEXP])
        rank_tab = sb("rank_tab", [P, TB, COLS])
        gate_tab = sb("gate_tab", [P, TB, COLS])
        ex = sb("ex", [P, 3, NEXP])
        exh = sb("exh", [P, EXTRA, NEXP])
        ext = sb("ext", [P, EXTRA, TB, NEXP])
        exr = sb("exr", [P, EXTRA, TB])
        startf = sb("startf", [P, DEPTH + 1])
        nf = sb("nf", [P, 2])
        start_i = sb("start_i", [P, DEPTH + 1], I32)
        n_i = sb("n_i", [P, DEPTH], I32)
        wide_i = sb("wide_i", [P, DEPTH * COLS], I32)
        expert_i = sb("expert_i", [P, DEPTH * COLS], I32)

        zflat = z[:].rearrange("p t c -> p (t c)")
        xg = zflat[:, 0:1024].rearrange("p (k s) -> p k s", k=KB)
        silu = zflat[:, 1024:2048]
        act = zflat[:, 2048:3072].rearrange("p (f s) -> p f s", f=KB)
        y = zflat[:, 3072:4096]
        place_gt = zflat[:, 4096:4352]
        place_tg = zflat[:, 4352:4608].rearrange("p (t s) -> p t s", t=TB)
        place_t = zflat[:, 4608:4864].rearrange("p (t s) -> p t s", t=TB)
        mixed = z[:, :, 0:D]

        lo = ctx.enter_context(nc.psum_tensor("lo", [P, 4, 512], F32))
        acc = ctx.enter_context(nc.psum_tensor("acc", [P, 4, 512], F32))
        lo_flat = lo[:].rearrange("p b c -> p (b c)")
        acc_tok = acc[:].rearrange("p (t b) c -> p t (b c)", t=TB)

        ident = cst[:, C_ID:C_ID + P]
        alpha_ident = cst[:, C_AID:C_AID + P]
        tri0 = cst[:, C_TRI0:C_TRI0 + SEQ]
        tri1 = cst[:, C_TRI1:C_TRI1 + SEQ]
        ones = cst[:, C_TRI0 + P:C_TRI0 + 2 * P]
        iota = cst[:, C_IOTA:C_IOTA + P]

        x_full, const_full = sem("x_full"), sem("const_full")
        ring_full = [sem(f"ring_full{i}") for i in range(SLOTS)]
        small_full, ln_full, wout_full, out_full = sem("small_full"), sem("ln_full"), sem("wout_full"), sem("out_full")
        ring_free = [sem(f"ring_free{i}") for i in range(SLOTS)]
        h_ready = sem("h_ready")
        turned = sem("turned")
        actT_ready = sem("actT_ready")
        forget_z = sem("forget_z")
        forget_arg = sem("forget_arg")
        forget_log = sem("forget_log")
        decay_ready = sem("decay_ready")
        cum_done = sem("cum_done")
        z_done = sem("z_done")
        z_rope = sem("z_rope")
        z_copied = sem("z_copied")
        z_rotated = sem("z_rotated")
        qkT_done = sem("qkT_done")
        qkT_ready = sem("qkT_ready")
        scores_done = sem("scores_done")
        masked_ready = sem("masked_ready")
        exp_done = sem("exp_done")
        probsT_done = sem("probsT_done")
        probsT_ready = sem("probsT_ready")
        inv_ready = sem("inv_ready")
        pv_done = sem("pv_done")
        mixed_done = sem("mixed_done")
        ssq_done = sem("ssq_done")
        ms_ready = sem("ms_ready")
        rms_root = sem("rms_root")
        rms_ready = sem("rms_ready")
        normed = sem("normed")
        proj_done = sem("proj_done")
        var_ready = sem("var_ready")
        ln_root = sem("ln_root")
        logits_done = sem("logits_done")
        shifted = sem("shifted")
        router_exp = sem("router_exp")
        sel_ready = sem("sel_ready")
        ranks_done = sem("ranks_done")
        plan_ready = sem("plan_ready")
        extras_ready = sem("extras_ready")
        dve_step = sem("dve_step")
        place_ready, gathered, xg_ready = sem("place_ready"), sem("gathered"), sem("xg_ready")
        gate_done, up_done, silu_done, act_ready = sem("gate_done"), sem("up_done"), sem("silu_done"), sem("act_ready")
        placeT_done, placeT_ready = sem("placeT_done"), sem("placeT_ready")
        down_done, y_ready, scattered = sem("down_done"), sem("y_ready"), sem("scattered")

        passed = sem("passed")

        x_v = x.rearrange("b (t p) d -> p (b t) d", p=P)
        out_v = out.rearrange("b (t p) d -> p (b t) d", p=P)
        w_in_v = w_in.rearrange("l (k p) n -> p l k n", p=P)
        w_out_v = w_out.rearrange("l (k p) n -> p l k n", p=P)
        wr_v = w_router.rearrange("(k p) e -> p k e", p=P)
        expert_v = [w.rearrange("l e (k p) f -> p l e k f", p=P) for w in (w_gate, w_up, w_down)]
        CONST_LOADS = 3

        block = ctx.enter_context(nc.Block())

        @block.sync
        def _(sp):
            for s in range(SLOTS):
                sp.sem_inc(ring_free[s], 1)
            sp.sem_inc(proj_done, 1)

            def load_item(layer, expert, turn):
                for s in range(SLOTS):
                    k = 2 * (s % 4)
                    sp.wait_ge(ring_free[s], turn)
                    src = expert_v[s // 4][:, bass.ds(layer, 1), bass.ds(expert, 1), k:k + 2, :]
                    sp.dma_start(ring[:, s, :], src.rearrange("p l e k f -> p (l e k) f")).then_inc(ring_full[s], 16)

            with sp.Fori(0, DEPTH) as l:
                sp.wait_ge(plan_ready, l + 1)
                sp.sem_inc(passed, 1)
                start = sp.value_load(start_i[0:1, bass.ds(l, 1)], min_val=0, max_val=19 * DEPTH)
                turn = sp.snap(start + l + 1)
                for c in range(N_CH):
                    for half in range(2):
                        s = 2 * c + half
                        sp.wait_ge(ring_free[s], turn)
                        src = w_in_v[:, bass.ds(l, 1), 4 * half:4 * half + 4, c * CH:(c + 1) * CH]
                        sp.dma_start(ring[:, s, :].rearrange("p (k n) -> p k n", k=4),
                                     src.rearrange("p l k n -> p (l k) n")).then_inc(ring_full[s], 16)
                sp.wait_ge(proj_done, l + 1)
                for q in range(4):
                    src = w_out_v[:, bass.ds(l, 1), 2 * q:2 * q + 2, :]
                    sp.dma_start(wout[:, 2 * q:2 * q + 2, :],
                                 src.rearrange("p l k n -> p (l k) n")).then_inc(wout_full, 16)
                with sp.Fori(0, NEXP) as j:
                    load_item(l, j, sp.snap(turn + 1 + j))
                sp.wait_ge(plan_ready, l + 2)
                sp.sem_inc(passed, 1)
                n = sp.value_load(n_i[0:1, bass.ds(l, 1)], min_val=NEXP, max_val=NEXP + EXTRA)
                with sp.If(n > NEXP):
                    sp.wait_ge(extras_ready, l + 1)
                    sp.sem_inc(passed, 1)
                    with sp.Fori(NEXP, n) as j:
                        e = sp.value_load(expert_i[0:1, bass.ds(l * COLS + j, 1)], min_val=0, max_val=NEXP - 1)
                        load_item(l, e, sp.snap(turn + 1 + j))
            sp.wait_ge(h_ready, 1 + 2 * DEPTH)
            sp.dma_start(out_v, h[:]).then_inc(out_full, 16)
            sp.wait_ge(out_full, 16)

        @block.gpsimd
        def _(pool):
            pool.dma_start(cst[:], consts).then_inc(const_full, 16)
            pool.dma_start(wr[:], wr_v).then_inc(const_full, 16)
            pool.dma_start(br[:, 0, :], b_router.partition_broadcast(P)).then_inc(const_full, 16)

            def load_small(layer):
                pool.dma_start(wf[:], w_in_v[:, bass.ds(layer, 1), :, ZF:ZF + N_FOX].rearrange("p l k n -> p (l k) n")
                               ).then_inc(small_full, 16)
                pool.dma_start(bf[:, 0, :], b_forget[bass.ds(layer, 1)].rearrange("l n -> (l n)").partition_broadcast(P)
                               ).then_inc(small_full, 16)
                pool.dma_start(gmix[:, 0:D_DIL // P], g_dil[bass.ds(layer, 1)].rearrange("l (k p) -> p (l k)", p=P)
                               ).then_inc(small_full, 16)
                pool.dma_start(gmix[:, D_DIL // P:KB], g_fox[bass.ds(layer, 1)].rearrange("l (k p) -> p (l k)", p=P)
                               ).then_inc(small_full, 16)

            def load_norm(layer, g, b):
                for i, v in enumerate((g, b)):
                    pool.dma_start(ln_gb[:, i, :], v[bass.ds(layer, 1)].rearrange("l d -> (l d)").partition_broadcast(P)
                                   ).then_inc(ln_full, 16)

            with nc.allow_non_contiguous_dma(reason="small vectors laid over the partitions"):
                load_small(0)
                with pool.Fori(0, DEPTH) as l:
                    pool.wait_ge(h_ready, 2 * l + 1)
                    pool.sem_inc(passed, 1)
                    load_norm(l, ln1_g, ln1_b)
                    pool.wait_ge(h_ready, 2 * l + 2)
                    pool.sem_inc(passed, 1)
                    load_norm(l, ln2_g, ln2_b)
                    with pool.If(l < DEPTH - 1):
                        load_small(nc.s_assert_within(l + 1, 1, DEPTH - 1))

        SMALL = 4 * 16

        @block.tensor
        def _(pe):
            def turn_h(l, src, first):
                for b in range(4):
                    for k in (2 * b, 2 * b + 1):
                        for t in range(TB):
                            at = (k % 2) * SEQ + t * P
                            mm = nc.tensor.transpose(lo[:, b, at:at + P], src[:, t, k * P:(k + 1) * P], ident)
                    mm.then_inc(turned, 1)

            def seed():
                for t in range(TB):
                    for half in range(2):
                        nc.tensor.matmul(acc[:, 2 * t + half, :], alpha_ident, h[:, t, half * 512:(half + 1) * 512],
                                         start=True, stop=False, skip_group_check=True)

            def turn_qk(l, p):
                if p >= 1:
                    pe.wait_ge(qkT_ready, l * PAIRS + p)
                cols = head_cols(2 * p)
                for i in range(4):
                    mm = nc.tensor.transpose(acc[:, 0, i * P:(i + 1) * P],
                                             z[:, i % 2, cols[i // 2]:cols[i // 2] + P], ident)
                mm.then_inc(qkT_done, 1)

            def scores(l, p):
                pe.wait_ge(qkT_ready, l * PAIRS + p + 1)
                for i in range(2):
                    hd = 2 * p + i
                    if hd >= 2:
                        pe.wait_ge(masked_ready, l * HEADS + hd - 1)
                    r = slice(i * HD, (i + 1) * HD)
                    qk = qkT[r, p % 2]
                    fox = hd >= N_DIL
                    f = hd - N_DIL
                    mm = nc.tensor.matmul(lo[:, i, 0:P], qk[:, 0, :], qk[:, 2, :], start=True, stop=not fox,
                                          skip_group_check=True)
                    mm = nc.tensor.matmul(lo[:, i, P:SKEYS], qk[:, 1, :], qk[:, 2:4, :].rearrange("p a b -> p (a b)"),
                                          start=False, stop=not fox, skip_group_check=True)
                    if fox:
                        nc.tensor.matmul(lo[:, i, 0:P], decay[:, 0, f, :], tri0[:, 0:P], start=False, stop=False,
                                         skip_group_check=True)
                        nc.tensor.matmul(lo[:, i, P:SKEYS], decay[:, 0, f, :], tri0, start=False, stop=False,
                                         skip_group_check=True)
                        mm = nc.tensor.matmul(lo[:, i, 2 * P:SKEYS], decay[:, 1, f, :], tri1[:, P:SEQ], start=False,
                                              stop=True, skip_group_check=True)
                    mm.then_inc(scores_done, 1)

            def turn_probs(l, p):
                for i in range(2):
                    hd = 2 * p + i
                    pe.wait_ge(exp_done, l * HEADS + hd + 1)
                    if hd >= 2:
                        pe.wait_ge(probsT_ready, l * HEADS + hd - 1)
                    for b in range(3):
                        mm = nc.tensor.transpose(lo[:, 2 + i, b * P:(b + 1) * P],
                                                 probs[:, hd % 4, b * P:(b + 1) * P], ident)
                    mm.then_inc(probsT_done, 1)

            def weigh_values(l, p):
                for i in range(2):
                    hd = 2 * p + i
                    v = head_cols(hd)[2]
                    pe.wait_ge(probsT_ready, l * HEADS + hd + 1)
                    if hd >= 2:
                        pe.wait_ge(mixed_done, l * HEADS + hd - 1)
                    nc.tensor.matmul(acc[:, 1 + i, 0:HD], probsT[:, i, 0:P], z[:, 0, v:v + HD],
                                     start=True, stop=True, skip_group_check=True)
                    nc.tensor.matmul(acc[:, 1 + i, HD:2 * HD], probsT[:, i, P:2 * P], z[:, 0, v:v + HD],
                                     start=False, stop=False, skip_group_check=True)
                    nc.tensor.matmul(acc[:, 1 + i, HD:2 * HD], probsT[:, i, 2 * P:3 * P], z[:, 1, v:v + HD],
                                     start=False, stop=True, skip_group_check=True).then_inc(pv_done, 1)

            def gather(turn):
                pe.wait_ge(place_ready, turn)
                for k in range(KB):
                    for t in range(TB):
                        mm = nc.tensor.matmul(lo[:, 2 + k // 4, (k % 4) * P:(k % 4 + 1) * P],
                                              h[:, t, k * P:(k + 1) * P], place_t[:, t, :],
                                              start=(k % 4 == 0 and t == 0), stop=(t == 1), skip_group_check=True)
                mm.then_inc(gathered, 1)

            def item(w, g, turn):
                full = pe.snap((turn + 1) * 16)
                for m, (done, bank) in enumerate(((gate_done, 0), (up_done, 2))):
                    for s in range(4):
                        pe.wait_ge(ring_full[4 * m + s], full)
                        for kk in range(2):
                            k = 2 * s + kk
                            for f in range(KB):
                                mm = nc.tensor.matmul(
                                    lo[:, bank + f // 4, (f % 4) * P:(f % 4) * P + w],
                                    ring[:, 4 * m + s, kk * D + f * P:kk * D + (f + 1) * P], xg[:, k, 0:w],
                                    start=(k == 0 and f % 4 == 0), stop=(k == KB - 1), skip_group_check=True)
                                if m == 1 and k == 0 and f == 0:
                                    mm.then_inc(ring_free[3], 1)
                        mm.then_inc(done if s == 3 else ring_free[4 * m + s], 1)
                a2 = pe.snap(g * 2)
                pe.wait_ge(silu_done, a2 + 2)
                for s in range(4):
                    if s % 2 == 0:
                        pe.wait_ge(act_ready, a2 + 1 + s // 2)
                    pe.wait_ge(ring_full[8 + s], full)
                    for kk in range(2):
                        f = 2 * s + kk
                        for half in range(2):
                            mm = nc.tensor.matmul(lo[0:w, half, :], act[:, f, 0:w],
                                                  ring[:, 8 + s, kk * D + half * 512:kk * D + (half + 1) * 512],
                                                  start=(f == 0), stop=(f == KB - 1), skip_group_check=True)
                            if f == 0 and half == 0:
                                mm.then_inc(ring_free[7], 1)
                    mm.then_inc(down_done if s == 3 else ring_free[8 + s], 1)
                    if s == 1:
                        for t in range(TB):
                            mm = nc.tensor.transpose(lo[0:w, 2, t * P:(t + 1) * P], place_tg[:, t, 0:w], ident)
                        mm.then_inc(placeT_done, 1)
                    if s == 2:
                        pe.wait_ge(placeT_ready, g + 1)
                        gather(turn + 1)
                pe.wait_ge(y_ready, a2 + 2)
                for t in range(TB):
                    for half in range(2):
                        mm = nc.tensor.matmul(acc[:, 2 * t + half, :], place_gt[0:w, t * P:(t + 1) * P],
                                              y[0:w, half * 512:(half + 1) * 512],
                                              start=False, stop=True, skip_group_check=True)
                        if t == 0 and half == 0:
                            mm.then_inc(ring_free[11], 1)
                mm.then_inc(scattered, 1)

            pe.wait_ge(const_full, 16 * CONST_LOADS)
            with pe.Fori(0, DEPTH) as l:
                pe.wait_ge(h_ready, 2 * l + 1)
                pe.wait_ge(plan_ready, l + 1)
                start = pe.value_load(start_i[0:1, bass.ds(l, 1)], min_val=0, max_val=19 * DEPTH)
                turn_h(l, h, 0)
                pe.wait_ge(actT_ready, l * 12 + 4)
                pe.wait_ge(small_full, l * SMALL + SMALL)
                for t in range(TB):
                    for k in range(KB):
                        mm = nc.tensor.matmul(acc[:, 1, t * N_FOX:(t + 1) * N_FOX], actT[:, k, t * P:(t + 1) * P],
                                              wf[:, k, :], start=(t == 0 and k == 0), stop=(k == KB - 1),
                                              skip_group_check=True)
                mm.then_inc(forget_z, 1)
                full = pe.snap((start + l + 1) * 16)
                for c in range(N_CH):
                    for t in range(TB):
                        n = TB * c + t
                        if 2 <= n < 2 + TB * ROPE_CH:
                            pe.wait_ge(z_rope, l * TB * ROPE_CH + n - 1)
                        elif n >= 2:
                            pe.wait_ge(z_copied, l * TB * (N_CH - ROPE_CH) + n - 1 - TB * ROPE_CH)
                        for k in range(KB):
                            if t == 0 and k % 4 == 0:
                                pe.wait_ge(ring_full[2 * c + k // 4], full)
                            mm = nc.tensor.matmul(acc[:, 2 + t, :], actT[:, k, t * P:(t + 1) * P],
                                                  ring[:, 2 * c + k // 4, (k % 4) * CH:(k % 4 + 1) * CH],
                                                  start=(k == 0), stop=(k == KB - 1))
                            if t == 1 and k == 3:
                                mm.then_inc(ring_free[2 * c], 1)
                            if t == 0 and k == 0 and c >= 1:
                                mm.then_inc(ring_free[2 * c - 1], 1)
                        mm.then_inc(z_done, 1)
                pe.wait_ge(decay_ready, l + 1)
                nc.tensor.matmul(acc[:, 1, 0:N_FOX], tri0[:, 0:P], fg[:, 5, 0, :], start=True, stop=True,
                                 skip_group_check=True).then_inc(ring_free[2 * N_CH - 1], 1)
                nc.tensor.matmul(acc[:, 1, N_FOX:2 * N_FOX], ones, fg[:, 5, 0, :], start=False, stop=False,
                                 skip_group_check=True)
                nc.tensor.matmul(acc[:, 1, N_FOX:2 * N_FOX], tri0[:, 0:P], fg[:, 5, 1, :], start=False, stop=True,
                                 skip_group_check=True).then_inc(cum_done, 1)
                pe.wait_ge(z_rotated, (l + 1) * TB * ROPE_CH)
                pe.wait_ge(z_copied, (l + 1) * TB * (N_CH - ROPE_CH))
                turn_qk(l, 0)
                for p in range(PAIRS + 1):
                    if p < PAIRS:
                        scores(l, p)
                    if p + 1 < PAIRS:
                        turn_qk(l, p + 1)
                    if p >= 1:
                        turn_probs(l, p - 1)
                        weigh_values(l, p - 1)
                pe.wait_ge(mixed_done, (l + 1) * HEADS)
                seed()
                pe.wait_ge(normed, 4 * l + 4)
                turn_h(l, mixed, 4)
                pe.wait_ge(actT_ready, l * 12 + 8)
                pe.wait_ge(wout_full, 64 * l + 64)
                for k in range(KB):
                    for t in range(TB):
                        for half in range(2):
                            mm = nc.tensor.matmul(acc[:, 2 * t + half, :], actT[:, k, t * P:(t + 1) * P],
                                                  wout[:, k, half * 512:(half + 1) * 512],
                                                  start=False, stop=(k == KB - 1), skip_group_check=True)
                mm.then_inc(proj_done, 1)
                pe.wait_ge(h_ready, 2 * l + 2)
                turn_h(l, h, 8)
                pe.wait_ge(actT_ready, l * 12 + 12)
                for t in range(TB):
                    for k in range(KB):
                        mm = nc.tensor.matmul(lo[:, 0, t * NEXP:(t + 1) * NEXP], actT[:, k, t * P:(t + 1) * P],
                                              wr[:, k, :], start=(t == 0 and k == 0), stop=(k == KB - 1),
                                              skip_group_check=True)
                mm.then_inc(logits_done, 1)
                seed()
                pe.wait_ge(sel_ready, l + 1)
                nc.tensor.matmul(lo[:, 1, 0:NEXP], tri0[:, 0:P], sel[:, 0, :], start=True, stop=True,
                                 skip_group_check=True)
                for at, mats in ((NEXP, (ones, tri0[:, 0:P])), (2 * NEXP, (ones, ones))):
                    for t in range(TB):
                        mm = nc.tensor.matmul(lo[:, 1, at:at + NEXP], mats[t], sel[:, t, :], start=False,
                                              stop=(t == 1), skip_group_check=True)
                mm.then_inc(ranks_done, 1)
                turn0 = pe.snap(start + l + 1)
                gather(turn0)
                pe.wait_ge(plan_ready, l + 2)
                n = pe.value_load(n_i[0:1, bass.ds(l, 1)], min_val=NEXP, max_val=NEXP + EXTRA)
                with pe.Fori(0, n) as j:
                    g = pe.snap(start + j)
                    turn = pe.snap(turn0 + j)
                    wide = pe.value_load(wide_i[0:1, bass.ds(l * COLS + j, 1)], min_val=0, max_val=1)
                    pe.wait_ge(xg_ready, turn)
                    with pe.If(wide > 0):
                        item(P, g, turn)
                    with pe.Else():
                        item(P // 2, g, turn)

        @block.scalar
        def _(a):
            def root(out_ap, in_ap):
                return nc.scalar.activation(out_ap, in_ap, ACT.Sqrt)

            a.dma_start(h[:], x_v).then_inc(x_full, 16)
            a.wait_ge(const_full, 16 * CONST_LOADS)
            with a.Fori(0, DEPTH) as l:
                a.wait_ge(plan_ready, l + 1)
                start = a.value_load(start_i[0:1, bass.ds(l, 1)], min_val=0, max_val=19 * DEPTH)
                for b in range(2):
                    a.wait_ge(turned, 12 * l + b + 1)
                    nc.scalar.copy(actT[:, 2 * b:2 * b + 2, :].rearrange("p k s -> p (k s)"), lo[:, b, :]
                                   ).then_inc(actT_ready, 1)
                a.wait_ge(forget_arg, l + 1)
                nc.scalar.activation(fg[:, 3], fg[:, 2], ACT.Exp).then_inc(forget_log, 1)
                a.wait_ge(forget_log, 2 * l + 1)
                nc.scalar.activation(fg[:, 4], fg[:, 3], ACT.Ln, bias=1.0).then_inc(forget_log, 1)
                for n in range(TB * ROPE_CH, TB * N_CH):
                    a.wait_ge(z_done, 12 * l + n + 1)
                    c, t = n // TB, n % TB
                    nc.scalar.copy(z[:, t, c * CH:(c + 1) * CH], acc[:, 2 + t, :]).then_inc(z_copied, 1)
                for p in range(PAIRS + 1):
                    if p == 0:
                        a.wait_ge(qkT_done, l * PAIRS + 1)
                        nc.scalar.copy(qkT[:, 0].rearrange("p a b -> p (a b)"), acc[:, 0, :]).then_inc(qkT_ready, 1)
                    if p + 1 < PAIRS:
                        a.wait_ge(qkT_done, l * PAIRS + p + 2)
                        nc.scalar.copy(qkT[:, (p + 1) % 2].rearrange("p a b -> p (a b)"), acc[:, 0, :]
                                       ).then_inc(qkT_ready, 1)
                    if p < PAIRS:
                        for i in range(2):
                            hd = 2 * p + i
                            a.wait_ge(masked_ready, l * HEADS + hd + 1)
                            if hd >= 4:
                                a.wait_ge(probsT_done, l * HEADS + hd - 3)
                            nc.scalar.activation(probs[:, hd % 4, 0:P], masked[:, i, 0:P], ACT.Exp,
                                                 bias=neg_max[:, hd % 4, 0:1], scale=1 / INV_SCALE,
                                                 accum_out=row_sum[:, hd % 4, 0:1])
                            nc.scalar.activation(probs[:, hd % 4, P:SKEYS], masked[:, i, P:SKEYS], ACT.Exp,
                                                 bias=neg_max[:, hd % 4, 1:2], scale=1 / INV_SCALE,
                                                 accum_out=row_sum[:, hd % 4, 1:2]).then_inc(exp_done, 1)
                    if p >= 1:
                        for i in range(2):
                            hd = 2 * (p - 1) + i
                            a.wait_ge(pv_done, l * HEADS + hd + 1)
                            a.wait_ge(inv_ready, l * HEADS + hd + 1)
                            for t in range(TB):
                                op = nc.scalar.mul(mixed[:, t, hd * HD:(hd + 1) * HD], acc[:, 1 + i, t * HD:(t + 1) * HD],
                                                   row_inv[:, i, t:t + 1])
                            op.then_inc(mixed_done, 1)
                a.wait_ge(mixed_done, (l + 1) * HEADS)
                for t in range(TB):
                    for gi, (c0, c1) in enumerate(((0, D_DIL), (D_DIL, D))):
                        nc.scalar.activation(probs[:].rearrange("p a b -> p (a b)")[:, 0:c1 - c0], mixed[:, t, c0:c1],
                                             ACT.Square, accum_out=ssq[:, t, gi:gi + 1]).then_inc(ssq_done, 1)
                        a.wait_ge(ssq_done, 4 * l + 2 * t + gi + 1)
                a.wait_ge(ms_ready, l + 1)
                root(rms[:, 1], rms[:, 0]).then_inc(rms_root, 1)
                a.wait_ge(rms_ready, l + 1)
                for gi, (c0, c1) in enumerate(((0, D_DIL), (D_DIL, D))):
                    nc.scalar.mul(mixed[:, 0, c0:c1], mixed[:, 0, c0:c1], rms[:, 2, 0, gi:gi + 1]).then_inc(normed, 1)
                for b in range(2):
                    a.wait_ge(turned, 12 * l + 4 + b + 1)
                    for k in (2 * b, 2 * b + 1):
                        op = nc.scalar.mul(actT[:, k, :], lo[:, b, (k % 2) * SEQ:(k % 2 + 1) * SEQ], gmix[:, k:k + 1])
                    op.then_inc(actT_ready, 1)
                a.wait_ge(var_ready, 2 * l + 1)
                root(lnt[:, 1], lnt[:, 0]).then_inc(ln_root, 1)
                for b in range(2):
                    a.wait_ge(turned, 12 * l + 8 + b + 1)
                    nc.scalar.copy(actT[:, 2 * b:2 * b + 2, :].rearrange("p k s -> p (k s)"), lo[:, b, :]
                                   ).then_inc(actT_ready, 1)
                a.wait_ge(shifted, l + 1)
                nc.scalar.activation(rt[:, 1], rt[:, 0], ACT.Exp).then_inc(router_exp, 1)
                a.wait_ge(plan_ready, l + 2)
                n = a.value_load(n_i[0:1, bass.ds(l, 1)], min_val=NEXP, max_val=NEXP + EXTRA)
                with a.Fori(0, n) as j:
                    g = a.snap(start + j)
                    a.wait_ge(gate_done, g + 1)
                    for b in range(2):
                        nc.scalar.activation(silu[:, b * 512:(b + 1) * 512], lo[:, b, :], ACT.Silu
                                             ).then_inc(silu_done, 1)
                    a.wait_ge(down_done, g + 1)
                    nc.scalar.copy(y[:, 0:512], lo[:, 0, :]).then_inc(y_ready, 1)
                a.wait_ge(var_ready, 2 * l + 2)
                root(lnt[:, 1], lnt[:, 0]).then_inc(ln_root, 1)

        @block.vector
        def _(v):
            DVE_STEPS = 77
            steps = [0]
            base = [0]

            def step(ins):
                steps[0] += 1
                ins.then_inc(dve_step, 1)
                v.wait_ge(dve_step, base[0] + steps[0])

            def layer_norm(l, which):
                for t in range(TB):
                    for half in range(2):
                        op = nc.vector.bn_stats(stats[:, t, half, :], acc[:, 2 * t + half, :])
                step(op)
                v.sem_inc(passed, 1)
                for t in range(TB):
                    op = nc.vector.bn_aggr(mv[:, t, :], stats[:, t].rearrange("p a b -> p (a b)"))
                step(op)
                nc.vector.tensor_scalar(lnt[:, 0], mv[:, :, 1], LN_EPS, None, ALU.add).then_inc(var_ready, 1)
                v.wait_ge(ln_full, 64 * l + 32 * (which + 1))
                for t in range(TB):
                    op = nc.vector.scalar_tensor_tensor(out=h[:, t, :], in0=acc_tok[:, t, :], scalar=mv[:, t, 0:1],
                                                        in1=ln_gb[:, 0, :], op0=ALU.subtract, op1=ALU.mult)
                v.wait_ge(ln_root, 2 * l + which + 1)
                step(nc.vector.reciprocal(lnt[:, 2], lnt[:, 1]))
                for t in range(TB):
                    op = nc.vector.scalar_tensor_tensor(out=h[:, t, :], in0=h[:, t, :], scalar=lnt[:, 2, t:t + 1],
                                                        in1=ln_gb[:, 1, :], op0=ALU.mult, op1=ALU.add)
                op.then_inc(h_ready, 1)

            def ranks(dst, src, n):
                vals = src.rearrange("p (n i) -> p n i", i=4)
                vj = vals.unsqueeze(2).to_broadcast([P, n, 4, 4])
                vi = vals.unsqueeze(3).to_broadcast([P, n, 4, 4])
                ca, cb = (cmp[:, i, 0:16 * n] for i in range(2))
                nc.vector.tensor_tensor(ca.rearrange("p (n i j) -> p n i j", i=4, j=4), vj, vi, ALU.is_gt)
                step(nc.vector.tensor_tensor(cb.rearrange("p (n i j) -> p n i j", i=4, j=4), vj, vi, ALU.is_ge))
                nc.vector.tensor_tensor(ca, ca, cst[:, C_UP:C_UP + 16 * n], ALU.mult)
                step(nc.vector.tensor_tensor(cb, cb, cst[:, C_LO:C_LO + 16 * n], ALU.mult))
                step(nc.vector.tensor_tensor(ca, ca, cb, ALU.add))
                step(nc.vector.tensor_reduce(dst, ca.rearrange("p (n j) -> p n j", j=4), AX.X, ALU.add))

            def place(col, turn):
                for t in range(TB):
                    nc.vector.tensor_scalar(place_t[:, t, :], iota, rank_tab[:, t, col], None, ALU.is_equal)
                for t in range(TB):
                    op = nc.vector.tensor_scalar(place_tg[:, t, :], iota, rank_tab[:, t, col], gate_tab[:, t, col],
                                                 ALU.is_equal, ALU.mult)
                op.then_inc(place_ready, 1)

            nc.vector.memset(startf[:], 0.0)
            nc.vector.memset(start_i[:], 0)
            nc.vector.memset(wide_i[:], 1)
            nc.vector.memset(rank_tab[:], 0.0)
            nc.vector.memset(gate_tab[:], 0.0).then_inc(plan_ready, 1)
            v.wait_ge(const_full, 16 * CONST_LOADS)
            v.wait_ge(x_full, 16)
            nc.vector.memset(nf[:], 0.0).then_inc(h_ready, 1)
            with v.Fori(0, DEPTH) as l:
                base[0] = v.snap(l * DVE_STEPS)
                v.wait_ge(plan_ready, l + 1)
                start = v.value_load(start_i[0:1, bass.ds(l, 1)], min_val=0, max_val=19 * DEPTH)
                for b in range(2, 4):
                    v.wait_ge(turned, 12 * l + b + 1)
                    nc.vector.tensor_copy(actT[:, 2 * b:2 * b + 2, :].rearrange("p k s -> p (k s)"), lo[:, b, :]
                                          ).then_inc(actT_ready, 1)
                v.wait_ge(forget_z, l + 1)
                step(nc.vector.tensor_tensor(fg[:, 0], acc[:, 1, 0:TB * N_FOX].rearrange("p (t n) -> p t n", t=TB),
                                             bf[:].to_broadcast([P, TB, N_FOX]), ALU.add))
                nc.vector.tensor_scalar(fg[:, 1], fg[:, 0], -1.0, 0.0, ALU.mult, ALU.max)
                nc.vector.scalar_tensor_tensor(out=fg[:, 2], in0=fg[:, 0], scalar=-1.0, in1=fg[:, 0], op0=ALU.mult,
                                               op1=ALU.min).then_inc(forget_arg, 1)
                for n in range(TB * ROPE_CH):
                    c, t = n // TB, n % TB
                    src = acc[:, 2 + t, :].rearrange("p (h two i) -> p h two i", two=2, i=32)
                    dst = z[:, t, c * CH:(c + 1) * CH].rearrange("p (h two i) -> p h two i", two=2, i=32)
                    cos, sin = (cst[:, C_COS + t * 64 + i * 32:C_COS + t * 64 + (i + 1) * 32].unsqueeze(1)
                                .to_broadcast([P, 8, 32]) for i in range(2))
                    t2sin = cmp[:, 0, :].rearrange("p (h i) -> p h i", i=32)
                    t1sin = cmp[:, 1, :].rearrange("p (h i) -> p h i", i=32)
                    v.wait_ge(z_done, 12 * l + n + 1)
                    nc.vector.tensor_tensor(dst[:, :, 0], src[:, :, 0], cos, ALU.mult)
                    nc.vector.tensor_tensor(t2sin, src[:, :, 1], sin, ALU.mult)
                    nc.vector.tensor_tensor(dst[:, :, 1], src[:, :, 1], cos, ALU.mult)
                    ins = nc.vector.tensor_tensor(t1sin, src[:, :, 0], sin, ALU.mult)
                    ins.then_inc(z_rope, 1)
                    v.wait_ge(z_rope, l * TB * ROPE_CH + n + 1)
                    nc.vector.tensor_tensor(dst[:, :, 0], dst[:, :, 0], t2sin, ALU.subtract)
                    nc.vector.tensor_tensor(dst[:, :, 1], dst[:, :, 1], t1sin, ALU.add).then_inc(z_rotated, 1)
                    v.wait_ge(z_rotated, l * TB * ROPE_CH + n + 1)
                v.wait_ge(forget_log, 2 * l + 2)
                step(nc.vector.tensor_tensor(fg[:, 6], fg[:, 1], fg[:, 4], ALU.add))
                step(nc.vector.tensor_scalar(fg[:, 5], fg[:, 6], INV_SCALE, None, ALU.mult))
                for t in range(TB):
                    for f in range(N_FOX):
                        op = nc.vector.tensor_scalar(decay[:, t, f, :], ones, fg[:, 5, t, f:f + 1], None, ALU.mult)
                op.then_inc(decay_ready, 1)
                v.wait_ge(cum_done, l + 1)
                step(nc.vector.tensor_copy(fg[:, 0].rearrange("p t n -> p (t n)"), acc[:, 1, 0:TB * N_FOX]))
                for p in range(PAIRS + 1):
                    if p < PAIRS:
                        for i in range(2):
                            hd = 2 * p + i
                            v.wait_ge(scores_done, l * HEADS + hd + 1)
                            if hd >= 2:
                                v.wait_ge(exp_done, l * HEADS + hd - 1)
                            if hd < N_DIL:
                                op = nc.vector.tensor_tensor(masked[:, i, :], lo[:, i, 0:SKEYS],
                                                             cst[:, C_MDIL:C_MDIL + SKEYS], ALU.add)
                            else:
                                f = hd - N_DIL
                                for t, (c0, c1) in enumerate(((0, P), (P, SKEYS))):
                                    op = nc.vector.scalar_tensor_tensor(
                                        out=masked[:, i, c0:c1], in0=lo[:, i, c0:c1], scalar=fg[:, 0, t, f:f + 1],
                                        in1=cst[:, C_MFOX + c0:C_MFOX + c1], op0=ALU.subtract, op1=ALU.add)
                            step(op)
                            nc.vector.tensor_reduce(row_max[:, i, 0:1], masked[:, i, 0:P], AX.X, ALU.max)
                            step(nc.vector.tensor_reduce(row_max[:, i, 1:2], masked[:, i, P:SKEYS], AX.X, ALU.max))
                            nc.vector.tensor_scalar(neg_max[:, hd % 4, :], row_max[:, i, :], -1 / INV_SCALE, None,
                                                    ALU.mult).then_inc(masked_ready, 1)
                    if p >= 1:
                        for i in range(2):
                            hd = 2 * (p - 1) + i
                            v.wait_ge(probsT_done, l * HEADS + hd + 1)
                            nc.vector.tensor_copy(probsT[:, i, :], lo[:, 2 + i, 0:SKEYS]).then_inc(probsT_ready, 1)
                            if hd >= 2:
                                v.wait_ge(mixed_done, l * HEADS + hd - 1)
                            nc.vector.reciprocal(row_inv[:, i, :], row_sum[:, hd % 4, :]).then_inc(inv_ready, 1)
                v.wait_ge(ssq_done, 4 * l + 4)
                nc.vector.tensor_scalar(rms[:, 0, :, 0], ssq[:, :, 0], 1.0 / D_DIL, RMS_EPS, ALU.mult, ALU.add)
                nc.vector.tensor_scalar(rms[:, 0, :, 1], ssq[:, :, 1], 1.0 / D_FOX, RMS_EPS, ALU.mult, ALU.add
                                        ).then_inc(ms_ready, 1)
                v.wait_ge(rms_root, l + 1)
                nc.vector.reciprocal(rms[:, 2], rms[:, 1]).then_inc(rms_ready, 1)
                v.wait_ge(rms_ready, l + 1)
                for gi, (c0, c1) in enumerate(((0, D_DIL), (D_DIL, D))):
                    nc.vector.tensor_scalar(mixed[:, 1, c0:c1], mixed[:, 1, c0:c1], rms[:, 2, 1, gi:gi + 1], None,
                                            ALU.mult).then_inc(normed, 1)
                for b in range(2, 4):
                    v.wait_ge(turned, 12 * l + 4 + b + 1)
                    for k in (2 * b, 2 * b + 1):
                        op = nc.vector.tensor_scalar(actT[:, k, :], lo[:, b, (k % 2) * SEQ:(k % 2 + 1) * SEQ],
                                                     gmix[:, k:k + 1], None, ALU.mult)
                    op.then_inc(actT_ready, 1)
                v.wait_ge(proj_done, l + 2)
                layer_norm(l, 0)
                for b in range(2, 4):
                    v.wait_ge(turned, 12 * l + 8 + b + 1)
                    nc.vector.tensor_copy(actT[:, 2 * b:2 * b + 2, :].rearrange("p k s -> p (k s)"), lo[:, b, :]
                                          ).then_inc(actT_ready, 1)
                v.wait_ge(logits_done, l + 1)
                step(nc.vector.tensor_tensor(rt[:, 2], lo[:, 0, 0:TB * NEXP].rearrange("p (t e) -> p t e", t=TB),
                                             br[:].to_broadcast([P, TB, NEXP]), ALU.add))
                step(nc.vector.tensor_reduce(r2[:, 0], rt[:, 2], AX.X, ALU.max))
                nc.vector.tensor_tensor(rt[:, 0], rt[:, 2], r2[:, 0].unsqueeze(2).to_broadcast([P, TB, NEXP]),
                                        ALU.subtract).then_inc(shifted, 1)
                v.wait_ge(router_exp, l + 1)
                step(nc.vector.tensor_reduce(r2[:, 1], rt[:, 1], AX.X, ALU.add))
                step(nc.vector.reciprocal(r2[:, 2], r2[:, 1]))
                step(nc.vector.tensor_tensor(rt[:, 2], rt[:, 1], r2[:, 2].unsqueeze(2).to_broadcast([P, TB, NEXP]),
                                             ALU.mult))
                probs16 = rt[:, 2].rearrange("p t e -> p (t e)")
                in_grp = rt[:, 3].rearrange("p t e -> p (t e)")
                ranks(in_grp, probs16, 8)
                best = rt[:, 4].rearrange("p t e -> p (t e)")
                step(nc.vector.scalar_tensor_tensor(out=best, in0=in_grp, scalar=1.5, in1=probs16, op0=ALU.is_lt,
                                                    op1=ALU.mult))
                step(nc.vector.tensor_reduce(r8[:, 0], best.rearrange("p (g i) -> p g i", i=4), AX.X, ALU.add))
                ranks(r8[:, 1], r8[:, 0], 2)
                step(nc.vector.tensor_scalar(r8[:, 2], r8[:, 1], 0.5, None, ALU.is_lt))
                chosen = r8[:, 2].unsqueeze(2).to_broadcast([P, 8, 4])
                nc.vector.scalar_tensor_tensor(out=sel[:].rearrange("p t (g i) -> p (t g) i", i=4),
                                               in0=in_grp.rearrange("p (g i) -> p g i", i=4), scalar=1.5, in1=chosen,
                                               op0=ALU.is_lt, op1=ALU.mult).then_inc(sel_ready, 1)
                step(nc.vector.tensor_tensor(rt[:, 5].rearrange("p t (g i) -> p (t g) i", i=4),
                                             best.rearrange("p (g i) -> p g i", i=4), chosen, ALU.mult))
                step(nc.vector.tensor_reduce(r2[:, 3], rt[:, 5], AX.X, ALU.add))
                step(nc.vector.reciprocal(r2[:, 4], r2[:, 3]))
                nc.vector.tensor_tensor(gate_tab[:, :, 0:NEXP], rt[:, 5],
                                        r2[:, 4].unsqueeze(2).to_broadcast([P, TB, NEXP]), ALU.mult)
                v.wait_ge(ranks_done, l + 1)
                step(nc.vector.tensor_tensor(rank_tab[:, :, 0:NEXP],
                                             lo[:, 1, 0:TB * NEXP].rearrange("p (t e) -> p t e", t=TB), sel[:],
                                             ALU.mult))
                turn0 = v.snap(start + l + 1)
                place(slice(0, 1), turn0)
                count = lo[:, 1, 2 * NEXP:3 * NEXP]
                nc.vector.tensor_scalar(wide_i[:, bass.ds(l * COLS, NEXP)], count, P / 2 + 0.5, None, ALU.is_gt)
                step(nc.vector.tensor_scalar(ex[:, 0], count, P + 0.5, None, ALU.is_gt))
                step(nc.vector.tensor_reduce(nf[:, 0:1], ex[:, 0], AX.X, ALU.add))
                step(nc.vector.tensor_scalar(nf[:, 1:2], nf[:, 0:1], float(NEXP), None, ALU.add))
                nc.vector.tensor_copy(n_i[:, bass.ds(l, 1)], nf[:, 1:2])
                step(nc.vector.tensor_tensor(startf[:, bass.ds(l + 1, 1)], startf[:, bass.ds(l, 1)], nf[:, 1:2],
                                             ALU.add))
                nc.vector.tensor_copy(start_i[:, bass.ds(l + 1, 1)], startf[:, bass.ds(l + 1, 1)]
                                      ).then_inc(plan_ready, 1)
                v.wait_ge(gathered, turn0)
                for b in range(2):
                    op = nc.vector.tensor_copy(xg[:, 4 * b:4 * b + 4, :].rearrange("p k s -> p (k s)"), lo[:, 2 + b, :])
                op.then_inc(xg_ready, 1)
                step(nc.vector.tensor_tensor(cmp[:, 0, :].rearrange("p (e f) -> p e f", e=NEXP),
                                             cst[:, C_L16:C_L16 + 256].rearrange("p (e f) -> p e f", e=NEXP),
                                             ex[:, 0].unsqueeze(1).to_broadcast([P, NEXP, NEXP]), ALU.mult))
                step(nc.vector.tensor_reduce(ex[:, 1], cmp[:, 0, :].rearrange("p (e f) -> p e f", e=NEXP), AX.X,
                                             ALU.add))
                for i in range(EXTRA):
                    op = nc.vector.scalar_tensor_tensor(out=exh[:, i, :], in0=ex[:, 1], scalar=float(i), in1=ex[:, 0],
                                                        op0=ALU.is_equal, op1=ALU.mult)
                step(op)
                for tab, shift in ((rank_tab, -float(P)), (gate_tab, 0.0)):
                    for i in range(EXTRA):
                        op = nc.vector.tensor_tensor(ext[:, i], tab[:, :, 0:NEXP],
                                                     exh[:, i:i + 1, :].to_broadcast([P, TB, NEXP]), ALU.mult)
                    step(op)
                    step(nc.vector.tensor_reduce(exr[:], ext[:], AX.X, ALU.add))
                    step(nc.vector.tensor_scalar(tab[:, :, NEXP:NEXP + EXTRA].rearrange("p t x -> p x t"), exr[:],
                                                 shift, None, ALU.add))
                step(nc.vector.tensor_tensor(ext[:, :, 0, :], exh[:],
                                             cst[:, C_E:C_E + NEXP].unsqueeze(1).to_broadcast([P, EXTRA, NEXP]),
                                             ALU.mult))
                step(nc.vector.tensor_reduce(exr[:, :, 0:1], ext[:, :, 0, :], AX.X, ALU.add))
                nc.vector.tensor_copy(expert_i[:, bass.ds(l * COLS + NEXP, EXTRA)], exr[:, :, 0]
                                      ).then_inc(extras_ready, 1)
                v.wait_ge(extras_ready, l + 1)
                v.sem_inc(passed, 1)
                n = v.value_load(n_i[0:1, bass.ds(l, 1)], min_val=NEXP, max_val=NEXP + EXTRA)
                with v.Fori(0, n) as j:
                    g = v.snap(start + j)
                    g2 = v.snap(g * 2)
                    turn = v.snap(turn0 + j)
                    v.wait_ge(up_done, g + 1)
                    for b in range(2):
                        v.wait_ge(silu_done, g2 + 1 + b)
                        nc.vector.tensor_tensor(act[:, 4 * b:4 * b + 4, :].rearrange("p f s -> p (f s)"),
                                                lo[:, 2 + b, :], silu[:, b * 512:(b + 1) * 512], ALU.mult
                                                ).then_inc(act_ready, 1)
                    v.wait_ge(placeT_done, g + 1)
                    nc.vector.tensor_copy(place_gt, lo[:, 2, 0:SEQ]).then_inc(placeT_ready, 1)
                    place(bass.ds(j + 1, 1), turn)
                    v.wait_ge(gathered, turn + 1)
                    for b in range(2):
                        op = nc.vector.tensor_copy(xg[:, 4 * b:4 * b + 4, :].rearrange("p k s -> p (k s)"),
                                                   lo[:, 2 + b, :])
                    op.then_inc(xg_ready, 1)
                    v.wait_ge(down_done, g + 1)
                    nc.vector.tensor_copy(y[:, 512:1024], lo[:, 1, :]).then_inc(y_ready, 1)
                v.wait_ge(scattered, start + n)
                layer_norm(l, 1)
            assert steps[0] == DVE_STEPS, steps[0]


_INS = ['x', 'w_in', 'b_forget', 'g_dil', 'g_fox', 'w_out', 'ln1_g', 'ln1_b', 'w_router', 'b_router',
        'w_gate', 'w_up', 'w_down', 'ln2_g', 'ln2_b']


def kernel(**inputs):
    import numpy as _np
    import concourse.bacc as _bacc
    from concourse import mybir as _mybir
    from concourse.bass_utils import run_bass_kernel_spmd as _run

    nc = _bacc.Bacc("TRN2", target_bir_lowering=False, num_devices=1, dynamic_dma_scratch_size=8192)
    arrays, args = {}, []
    for name in _INS + ['consts']:
        a = constants() if name == 'consts' else _np.ascontiguousarray(inputs[name])
        arrays[f"in_{name}_dram"] = a
        args.append(nc.dram_tensor(f"in_{name}_dram", a.shape, _mybir.dt.from_np(a.dtype), kind="ExternalInput").ap())
    args.append(nc.dram_tensor("out_dram", (1, SEQ, D), F32, kind="ExternalOutput").ap())
    build(nc, *args)
    r = _run(nc, [arrays], core_ids=[0])
    return r.results[0]["out_dram"]
```

```python
from contextlib import ExitStack

import numpy as np

import concourse.bass as bass
from concourse import mybir

ALU = mybir.AluOpType
ACT = mybir.ActivationFunctionType
AX = mybir.AxisListType
F32 = mybir.dt.float32
I32 = mybir.dt.int32

P = 128
DEPTH, SEQ, D = 2, 256, 1024
HD = 64
N_DIL, N_FOX = 12, 4
HEADS = N_DIL + N_FOX
PAIRS = HEADS // 2
D_DIL, D_FOX = N_DIL * HD, N_FOX * HD
Q_DIL, K_DIL, V_DIL = 0, D_DIL, 2 * D_DIL
Q_FOX = 3 * D_DIL
K_FOX, V_FOX = Q_FOX + D_FOX, Q_FOX + 2 * D_FOX
ZF = V_FOX + D_FOX
TB = SEQ // P
KB = D // P
CH = 512
N_CH = ZF // CH
ROPE_CH = 2 * D_DIL // CH
NEXP, NGRP, EPG = 16, 4, 4
W = 64
MOST = NEXP + 2 * SEQ // W
ITEMS = MOST + 1
SLOTS = 12
TURNS = NEXP + 1
ALPHA = (2.0 * DEPTH) ** 0.25
LN_EPS, RMS_EPS = 1e-5, 1e-6
INV_SCALE = 8.0
NEG = -1e30
SKEYS = P + SEQ

C_ID, C_AID = 0, P
C_TRI0, C_TRI1 = 2 * P, 2 * P + SEQ
C_MDIL = C_TRI1 + SEQ
C_MFOX = C_MDIL + SKEYS
C_COS = C_MFOX + SKEYS
C_IOTA = C_COS + TB * 2 * 32
C_UP = C_IOTA + SEQ
C_LO = C_UP + 8 * 16
C_L16 = C_LO + 8 * 16
C_END = C_L16 + NEXP * NEXP


def constants():
    t = np.zeros((P, C_END), np.float32)
    p = np.arange(P)
    t[:, C_ID:C_ID + P] = np.eye(P)
    t[:, C_AID:C_AID + P] = np.eye(P) * ALPHA
    j = np.arange(SEQ)
    t[:, C_TRI0:C_TRI0 + SEQ] = p[:, None] <= j[None]
    t[:, C_TRI1:C_TRI1 + SEQ] = p[:, None] + P <= j[None]
    for b in range(TB):
        keys = np.arange(P * (b + 1))
        delta = (p[:, None] + b * P) - keys[None]
        ok = delta >= 0
        n = (ok & (delta <= 128)) * 1.0 + (ok & (delta % 4 == 0)) + (ok & (delta % 16 == 0))
        at = b * P
        bias = np.where(n > 0, INV_SCALE * np.log(np.maximum(n, 1)), NEG)
        t[:, C_MDIL + at:C_MDIL + at + len(keys)] = bias
        t[:, C_MFOX + at:C_MFOX + at + len(keys)] = np.where(ok, 0.0, NEG)
        inv = (np.float32(10000.0) ** (-np.arange(32, dtype=np.float32) / np.float32(32))).astype(np.float32)
        ang = ((p + b * P).astype(np.float32)[:, None] * inv[None]).astype(np.float32)
        t[:, C_COS + b * 64:C_COS + b * 64 + 32] = np.cos(ang)
        t[:, C_COS + b * 64 + 32:C_COS + b * 64 + 64] = np.sin(ang)
    t[:, C_IOTA:C_IOTA + SEQ] = np.arange(1, SEQ + 1)
    i4 = np.arange(4)
    t[:, C_UP:C_UP + 128] = np.tile((i4[None] > i4[:, None]).astype(np.float32).ravel(), 8)
    t[:, C_LO:C_LO + 128] = np.tile((i4[None] < i4[:, None]).astype(np.float32).ravel(), 8)
    e = np.arange(NEXP)
    t[:, C_L16:C_L16 + 256] = (e[None] <= e[:, None]).astype(np.float32).ravel()
    return t


def head_cols(h):
    if h < N_DIL:
        return Q_DIL + h * HD, K_DIL + h * HD, V_DIL + h * HD
    return Q_FOX + (h - N_DIL) * HD, K_FOX + (h - N_DIL) * HD, V_FOX + (h - N_DIL) * HD


def build(nc, x, w_in, b_forget, g_dil, g_fox, w_out, ln1_g, ln1_b, w_router, b_router,
          w_gate, w_up, w_down, ln2_g, ln2_b, consts, out):
    with ExitStack() as ctx:
        def sb(name, shape, dt=F32):
            return ctx.enter_context(nc.sbuf_tensor(name, shape, dt))

        def sem(name):
            return ctx.enter_context(nc.semaphore(name))

        ring = sb("ring", [P, SLOTS, 2048])
        wout = sb("wout", [P, KB, D])
        cst = sb("cst", [P, C_END])
        h = sb("h", [P, TB, D])
        actT = sb("actT", [P, KB, SEQ])
        z = sb("z", [P, TB, ZF])
        qkT = sb("qkT", [P, 2, 4, P])
        masked = sb("masked", [P, 2, SKEYS])
        probs = sb("probs", [P, 4, SKEYS])
        probsT = sb("probsT", [P, 2, SKEYS])
        decay = sb("decay", [P, TB, N_FOX, P])
        ln_gb = sb("ln_gb", [P, 2, D])
        wf = sb("wf", [P, KB, N_FOX])
        bf = sb("bf", [P, 1, N_FOX])
        gmix = sb("gmix", [P, KB])
        wr = sb("wr", [P, KB, NEXP])
        br = sb("br", [P, 1, NEXP])
        fg = sb("fg", [P, 7, TB, N_FOX])
        row_max = sb("row_max", [P, 2, TB])
        neg_max = sb("neg_max", [P, 4, TB])
        row_sum = sb("row_sum", [P, 4, TB])
        row_inv = sb("row_inv", [P, 2, TB])
        ssq = sb("ssq", [P, TB, 2])
        rms = sb("rms", [P, 3, TB, 2])
        stats = sb("stats", [P, TB, 2, 6])
        mv = sb("mv", [P, TB, 2])
        lnt = sb("lnt", [P, 3, TB])
        rt = sb("rt", [P, 6, TB, NEXP])
        r8 = sb("r8", [P, 6, 8])
        r2 = sb("r2", [P, 5, TB])
        cmp = probs[:].rearrange("p a b -> p (a b)")[:, 0:512].rearrange("p (a b) -> p a b", a=2)
        sel = sb("sel", [P, TB, NEXP])
        rank_tab = sb("rank_tab", [P, TB, NEXP])
        gate_tab = sb("gate_tab", [P, TB, NEXP])
        nsub = sb("nsub", [P, 2, NEXP])
        itab = sb("itab", [P, 4, ITEMS])
        startf = sb("startf", [P, DEPTH + 1])
        start_i = sb("start_i", [P, DEPTH + 1], I32)
        n_i = sb("n_i", [P, DEPTH], I32)
        expert_i = sb("expert_i", [P, DEPTH * ITEMS], I32)
        block_i = sb("block_i", [P, DEPTH * ITEMS], I32)
        last_i = sb("last_i", [P, DEPTH * ITEMS], I32)

        zflat = z[:].rearrange("p t c -> p (t c)")
        xg = zflat[:, 0:512].rearrange("p (k s) -> p k s", k=KB)
        silu = zflat[:, 512:1024]
        act = zflat[:, 1024:1536]
        act_t = zflat[:, 1536:2048].rearrange("p (b half s) -> p b half s", b=4, half=2)
        y = zflat[:, 2048:2560]
        place_gt = zflat[:, 2560:2816]
        place_tg = zflat[:, 2816:3072].rearrange("p (t two s) -> p t two s", t=TB, two=2)
        place_t = zflat[:, 3072:3328].rearrange("p (t two s) -> p t two s", t=TB, two=2)
        mixed = z[:, :, 0:D]

        lo = ctx.enter_context(nc.psum_tensor("lo", [P, 4, 512], F32))
        acc = ctx.enter_context(nc.psum_tensor("acc", [P, 4, 512], F32))
        lo_flat = lo[:].rearrange("p b c -> p (b c)")
        acc_tok = acc[:].rearrange("p (t b) c -> p t (b c)", t=TB)

        ident = cst[:, C_ID:C_ID + P]
        alpha_ident = cst[:, C_AID:C_AID + P]
        tri0 = cst[:, C_TRI0:C_TRI0 + SEQ]
        tri1 = cst[:, C_TRI1:C_TRI1 + SEQ]
        ones = cst[:, C_TRI0 + P:C_TRI0 + 2 * P]
        iota = cst[:, C_IOTA:C_IOTA + SEQ]
        pscratch = probs[:].rearrange("p a b -> p (a b)")

        x_full, const_full = sem("x_full"), sem("const_full")
        ring_full = [sem(f"ring_full{i}") for i in range(SLOTS)]
        small_full, ln_full, wout_full, out_full = sem("small_full"), sem("ln_full"), sem("wout_full"), sem("out_full")
        ring_free = [sem(f"ring_free{i}") for i in range(SLOTS)]
        h_ready = sem("h_ready")
        turned = sem("turned")
        actT_ready = sem("actT_ready")
        forget_z = sem("forget_z")
        forget_arg = sem("forget_arg")
        forget_log = sem("forget_log")
        decay_ready = sem("decay_ready")
        cum_done = sem("cum_done")
        z_done = sem("z_done")
        z_rope = sem("z_rope")
        z_copied = sem("z_copied")
        z_rotated = sem("z_rotated")
        qkT_done = sem("qkT_done")
        qkT_ready = sem("qkT_ready")
        scores_done = sem("scores_done")
        masked_ready = sem("masked_ready")
        exp_done = sem("exp_done")
        probsT_done = sem("probsT_done")
        probsT_ready = sem("probsT_ready")
        inv_ready = sem("inv_ready")
        pv_done = sem("pv_done")
        mixed_done = sem("mixed_done")
        ssq_done = sem("ssq_done")
        ms_ready = sem("ms_ready")
        rms_root = sem("rms_root")
        rms_ready = sem("rms_ready")
        normed = sem("normed")
        proj_done = sem("proj_done")
        var_ready = sem("var_ready")
        ln_root = sem("ln_root")
        logits_done = sem("logits_done")
        shifted = sem("shifted")
        router_exp = sem("router_exp")
        sel_ready = sem("sel_ready")
        ranks_done = sem("ranks_done")
        plan_ready = sem("plan_ready")
        dve_step = sem("dve_step")
        place_ready, gathered, xg_ready = sem("place_ready"), sem("gathered"), sem("xg_ready")
        gate_done, up_done, silu_done, act_ready = sem("gate_done"), sem("up_done"), sem("silu_done"), sem("act_ready")
        act_turned, act_t_ready = sem("act_turned"), sem("act_t_ready")
        placeT_done, placeT_ready = sem("placeT_done"), sem("placeT_ready")
        down_done, y_ready, scattered = sem("down_done"), sem("y_ready"), sem("scattered")

        passed = sem("passed")

        x_v = x.rearrange("b (t p) d -> p (b t) d", p=P)
        out_v = out.rearrange("b (t p) d -> p (b t) d", p=P)
        w_in_v = w_in.rearrange("l (k p) n -> p l k n", p=P)
        w_out_v = w_out.rearrange("l (k p) n -> p l k n", p=P)
        wr_v = w_router.rearrange("(k p) e -> p k e", p=P)
        expert_v = [w.rearrange("l e (k p) f -> p l e k f", p=P) for w in (w_gate, w_up, w_down)]
        CONST_LOADS = 3

        block = ctx.enter_context(nc.Block())

        @block.sync
        def _(sp):
            for s in range(SLOTS):
                sp.sem_inc(ring_free[s], 1)
            sp.sem_inc(proj_done, 1)

            def load_item(layer, expert, turn):
                for s in range(SLOTS):
                    k = 2 * (s % 4)
                    sp.wait_ge(ring_free[s], turn)
                    src = expert_v[s // 4][:, bass.ds(layer, 1), bass.ds(expert, 1), k:k + 2, :]
                    sp.dma_start(ring[:, s, :], src.rearrange("p l e k f -> p (l e k) f")).then_inc(ring_full[s], 16)

            with sp.Fori(0, DEPTH) as l:
                turn = sp.snap(l * TURNS + 1)
                for c in range(N_CH):
                    for half in range(2):
                        s = 2 * c + half
                        sp.wait_ge(ring_free[s], turn)
                        src = w_in_v[:, bass.ds(l, 1), 4 * half:4 * half + 4, c * CH:(c + 1) * CH]
                        sp.dma_start(ring[:, s, :].rearrange("p (k n) -> p k n", k=4),
                                     src.rearrange("p l k n -> p (l k) n")).then_inc(ring_full[s], 16)
                sp.wait_ge(proj_done, l + 1)
                for q in range(4):
                    src = w_out_v[:, bass.ds(l, 1), 2 * q:2 * q + 2, :]
                    sp.dma_start(wout[:, 2 * q:2 * q + 2, :],
                                 src.rearrange("p l k n -> p (l k) n")).then_inc(wout_full, 16)
                with sp.Fori(0, NEXP) as j:
                    load_item(l, j, sp.snap(turn + 1 + j))
            sp.wait_ge(h_ready, 1 + 2 * DEPTH)
            sp.dma_start(out_v, h[:]).then_inc(out_full, 16)
            sp.wait_ge(out_full, 16)

        @block.gpsimd
        def _(pool):
            pool.dma_start(cst[:], consts).then_inc(const_full, 16)
            pool.dma_start(wr[:], wr_v).then_inc(const_full, 16)
            pool.dma_start(br[:, 0, :], b_router.partition_broadcast(P)).then_inc(const_full, 16)

            def load_small(layer):
                pool.dma_start(wf[:], w_in_v[:, bass.ds(layer, 1), :, ZF:ZF + N_FOX].rearrange("p l k n -> p (l k) n")
                               ).then_inc(small_full, 16)
                pool.dma_start(bf[:, 0, :], b_forget[bass.ds(layer, 1)].rearrange("l n -> (l n)").partition_broadcast(P)
                               ).then_inc(small_full, 16)
                pool.dma_start(gmix[:, 0:D_DIL // P], g_dil[bass.ds(layer, 1)].rearrange("l (k p) -> p (l k)", p=P)
                               ).then_inc(small_full, 16)
                pool.dma_start(gmix[:, D_DIL // P:KB], g_fox[bass.ds(layer, 1)].rearrange("l (k p) -> p (l k)", p=P)
                               ).then_inc(small_full, 16)

            def load_norm(layer, g, b):
                for i, v in enumerate((g, b)):
                    pool.dma_start(ln_gb[:, i, :], v[bass.ds(layer, 1)].rearrange("l d -> (l d)").partition_broadcast(P)
                                   ).then_inc(ln_full, 16)

            with nc.allow_non_contiguous_dma(reason="small vectors laid over the partitions"):
                load_small(0)
                with pool.Fori(0, DEPTH) as l:
                    pool.wait_ge(h_ready, 2 * l + 1)
                    pool.sem_inc(passed, 1)
                    load_norm(l, ln1_g, ln1_b)
                    pool.wait_ge(h_ready, 2 * l + 2)
                    pool.sem_inc(passed, 1)
                    load_norm(l, ln2_g, ln2_b)
                    with pool.If(l < DEPTH - 1):
                        load_small(nc.s_assert_within(l + 1, 1, DEPTH - 1))

        SMALL = 4 * 16

        @block.tensor
        def _(pe):
            def turn_h(l, src, first):
                for b in range(4):
                    for k in (2 * b, 2 * b + 1):
                        for t in range(TB):
                            at = (k % 2) * SEQ + t * P
                            mm = nc.tensor.transpose(lo[:, b, at:at + P], src[:, t, k * P:(k + 1) * P], ident)
                    mm.then_inc(turned, 1)

            def seed():
                for t in range(TB):
                    for half in range(2):
                        nc.tensor.matmul(acc[:, 2 * t + half, :], alpha_ident, h[:, t, half * 512:(half + 1) * 512],
                                         start=True, stop=False, skip_group_check=True)

            def turn_qk(l, p):
                if p >= 1:
                    pe.wait_ge(qkT_ready, l * PAIRS + p)
                cols = head_cols(2 * p)
                for i in range(4):
                    mm = nc.tensor.transpose(acc[:, 0, i * P:(i + 1) * P],
                                             z[:, i % 2, cols[i // 2]:cols[i // 2] + P], ident)
                mm.then_inc(qkT_done, 1)

            def scores(l, p):
                pe.wait_ge(qkT_ready, l * PAIRS + p + 1)
                for i in range(2):
                    hd = 2 * p + i
                    if hd >= 2:
                        pe.wait_ge(masked_ready, l * HEADS + hd - 1)
                    r = slice(i * HD, (i + 1) * HD)
                    qk = qkT[r, p % 2]
                    fox = hd >= N_DIL
                    f = hd - N_DIL
                    mm = nc.tensor.matmul(lo[:, i, 0:P], qk[:, 0, :], qk[:, 2, :], start=True, stop=not fox,
                                          skip_group_check=True)
                    mm = nc.tensor.matmul(lo[:, i, P:SKEYS], qk[:, 1, :], qk[:, 2:4, :].rearrange("p a b -> p (a b)"),
                                          start=False, stop=not fox, skip_group_check=True)
                    if fox:
                        nc.tensor.matmul(lo[:, i, 0:P], decay[:, 0, f, :], tri0[:, 0:P], start=False, stop=False,
                                         skip_group_check=True)
                        nc.tensor.matmul(lo[:, i, P:SKEYS], decay[:, 0, f, :], tri0, start=False, stop=False,
                                         skip_group_check=True)
                        mm = nc.tensor.matmul(lo[:, i, 2 * P:SKEYS], decay[:, 1, f, :], tri1[:, P:SEQ], start=False,
                                              stop=True, skip_group_check=True)
                    mm.then_inc(scores_done, 1)

            def turn_probs(l, p):
                for i in range(2):
                    hd = 2 * p + i
                    pe.wait_ge(exp_done, l * HEADS + hd + 1)
                    if hd >= 2:
                        pe.wait_ge(probsT_ready, l * HEADS + hd - 1)
                    for b in range(3):
                        mm = nc.tensor.transpose(lo[:, 2 + i, b * P:(b + 1) * P],
                                                 probs[:, hd % 4, b * P:(b + 1) * P], ident)
                    mm.then_inc(probsT_done, 1)

            def weigh_values(l, p):
                for i in range(2):
                    hd = 2 * p + i
                    v = head_cols(hd)[2]
                    pe.wait_ge(probsT_ready, l * HEADS + hd + 1)
                    if hd >= 2:
                        pe.wait_ge(mixed_done, l * HEADS + hd - 1)
                    nc.tensor.matmul(acc[:, 1 + i, 0:HD], probsT[:, i, 0:P], z[:, 0, v:v + HD],
                                     start=True, stop=True, skip_group_check=True)
                    nc.tensor.matmul(acc[:, 1 + i, HD:2 * HD], probsT[:, i, P:2 * P], z[:, 0, v:v + HD],
                                     start=False, stop=False, skip_group_check=True)
                    nc.tensor.matmul(acc[:, 1 + i, HD:2 * HD], probsT[:, i, 2 * P:3 * P], z[:, 1, v:v + HD],
                                     start=False, stop=True, skip_group_check=True).then_inc(pv_done, 1)

            def gather(turn, release=None):
                pe.wait_ge(place_ready, turn)
                for k in range(KB):
                    for t in range(TB):
                        mm = nc.tensor.matmul(lo[:, 2 + k // 4, (k % 4) * P:(k % 4 + 1) * P],
                                              h[:, t, k * P:(k + 1) * P],
                                              place_t[:, t].rearrange("p two s -> p (two s)"),
                                              start=(k % 4 == 0 and t == 0), stop=(t == 1), skip_group_check=True)
                        if release is not None and k == 0 and t == 0:
                            mm.then_inc(release, 1)
                mm.then_inc(gathered, 1)

            def halves(bank, lhsT, s, kk, start, stop):
                for half in range(2):
                    at = kk * D + half * 512
                    mm = nc.tensor.matmul(lo[half * W:(half + 1) * W, bank, :], lhsT, ring[:, s, at:at + 512],
                                          start=start, stop=stop, skip_group_check=True)
                return mm

            def item(last, full, g, turn):
                for m, done in enumerate((gate_done, up_done)):
                    for s in range(4):
                        pe.wait_ge(ring_full[4 * m + s], full)
                        for kk in range(2):
                            k = 2 * s + kk
                            mm = halves(m, xg[:, k, :], 4 * m + s, kk, k == 0, k == KB - 1)
                            if last and m == 1 and k == 0:
                                mm.then_inc(ring_free[3], 1)
                        if s == 3:
                            mm.then_inc(done, 1)
                        elif last:
                            mm.then_inc(ring_free[4 * m + s], 1)
                gather(turn + 1, ring_free[7] if last else None)
                pe.wait_ge(act_ready, g + 1)
                for b in range(4):
                    mm = nc.tensor.transpose(lo[:, 1, b * P:(b + 1) * P], act[:, b * P:(b + 1) * P], ident)
                mm.then_inc(act_turned, 1)
                pe.wait_ge(xg_ready, turn + 1)
                for t in range(TB):
                    mm = nc.tensor.transpose(lo[:, 2, t * P:(t + 1) * P],
                                             place_tg[:, t].rearrange("p two s -> p (two s)"), ident)
                mm.then_inc(placeT_done, 1)
                pe.wait_ge(act_t_ready, g + 1)
                for s in range(4):
                    pe.wait_ge(ring_full[8 + s], full)
                    for kk in range(2):
                        f = 2 * s + kk
                        mm = halves(0, act_t[:, f % 4, f // 4, :], 8 + s, kk, f == 0, f == KB - 1)
                    if s == 3:
                        mm.then_inc(down_done, 1)
                    elif last:
                        mm.then_inc(ring_free[8 + s], 1)
                pe.wait_ge(placeT_ready, g + 1)
                pe.wait_ge(y_ready, g + 1)
                for t in range(TB):
                    for half in range(2):
                        r = slice(half * W, (half + 1) * W)
                        mm = nc.tensor.matmul(acc[:, 2 * t + half, :], place_gt[r, t * P:(t + 1) * P], y[r, :],
                                              start=False, stop=True, skip_group_check=True)
                        if last and t == 0 and half == 0:
                            mm.then_inc(ring_free[11], 1)
                mm.then_inc(scattered, 1)

            pe.wait_ge(const_full, 16 * CONST_LOADS)
            with pe.Fori(0, DEPTH) as l:
                pe.wait_ge(h_ready, 2 * l + 1)
                pe.wait_ge(plan_ready, l + 1)
                start = pe.value_load(start_i[0:1, bass.ds(l, 1)], min_val=0, max_val=MOST * DEPTH)
                turn_h(l, h, 0)
                pe.wait_ge(actT_ready, l * 12 + 4)
                pe.wait_ge(small_full, l * SMALL + SMALL)
                for t in range(TB):
                    for k in range(KB):
                        mm = nc.tensor.matmul(acc[:, 1, t * N_FOX:(t + 1) * N_FOX], actT[:, k, t * P:(t + 1) * P],
                                              wf[:, k, :], start=(t == 0 and k == 0), stop=(k == KB - 1),
                                              skip_group_check=True)
                mm.then_inc(forget_z, 1)
                full = pe.snap(l * (16 * TURNS) + 16)
                for c in range(N_CH):
                    for t in range(TB):
                        n = TB * c + t
                        if 2 <= n < 2 + TB * ROPE_CH:
                            pe.wait_ge(z_rope, l * TB * ROPE_CH + n - 1)
                        elif n >= 2:
                            pe.wait_ge(z_copied, l * TB * (N_CH - ROPE_CH) + n - 1 - TB * ROPE_CH)
                        for k in range(KB):
                            if t == 0 and k % 4 == 0:
                                pe.wait_ge(ring_full[2 * c + k // 4], full)
                            mm = nc.tensor.matmul(acc[:, 2 + t, :], actT[:, k, t * P:(t + 1) * P],
                                                  ring[:, 2 * c + k // 4, (k % 4) * CH:(k % 4 + 1) * CH],
                                                  start=(k == 0), stop=(k == KB - 1))
                            if t == 1 and k == 3:
                                mm.then_inc(ring_free[2 * c], 1)
                            if t == 0 and k == 0 and c >= 1:
                                mm.then_inc(ring_free[2 * c - 1], 1)
                        mm.then_inc(z_done, 1)
                pe.wait_ge(decay_ready, l + 1)
                nc.tensor.matmul(acc[:, 1, 0:N_FOX], tri0[:, 0:P], fg[:, 5, 0, :], start=True, stop=True,
                                 skip_group_check=True).then_inc(ring_free[2 * N_CH - 1], 1)
                nc.tensor.matmul(acc[:, 1, N_FOX:2 * N_FOX], ones, fg[:, 5, 0, :], start=False, stop=False,
                                 skip_group_check=True)
                nc.tensor.matmul(acc[:, 1, N_FOX:2 * N_FOX], tri0[:, 0:P], fg[:, 5, 1, :], start=False, stop=True,
                                 skip_group_check=True).then_inc(cum_done, 1)
                pe.wait_ge(z_rotated, (l + 1) * TB * ROPE_CH)
                pe.wait_ge(z_copied, (l + 1) * TB * (N_CH - ROPE_CH))
                turn_qk(l, 0)
                for p in range(PAIRS + 1):
                    if p < PAIRS:
                        scores(l, p)
                    if p + 1 < PAIRS:
                        turn_qk(l, p + 1)
                    if p >= 1:
                        turn_probs(l, p - 1)
                        weigh_values(l, p - 1)
                pe.wait_ge(mixed_done, (l + 1) * HEADS)
                seed()
                pe.wait_ge(normed, 4 * l + 4)
                turn_h(l, mixed, 4)
                pe.wait_ge(actT_ready, l * 12 + 8)
                pe.wait_ge(wout_full, 64 * l + 64)
                for k in range(KB):
                    for t in range(TB):
                        for half in range(2):
                            mm = nc.tensor.matmul(acc[:, 2 * t + half, :], actT[:, k, t * P:(t + 1) * P],
                                                  wout[:, k, half * 512:(half + 1) * 512],
                                                  start=False, stop=(k == KB - 1), skip_group_check=True)
                mm.then_inc(proj_done, 1)
                pe.wait_ge(h_ready, 2 * l + 2)
                turn_h(l, h, 8)
                pe.wait_ge(actT_ready, l * 12 + 12)
                for t in range(TB):
                    for k in range(KB):
                        mm = nc.tensor.matmul(lo[:, 0, t * NEXP:(t + 1) * NEXP], actT[:, k, t * P:(t + 1) * P],
                                              wr[:, k, :], start=(t == 0 and k == 0), stop=(k == KB - 1),
                                              skip_group_check=True)
                mm.then_inc(logits_done, 1)
                seed()
                pe.wait_ge(sel_ready, l + 1)
                nc.tensor.matmul(lo[:, 1, 0:NEXP], tri0[:, 0:P], sel[:, 0, :], start=True, stop=True,
                                 skip_group_check=True)
                for at, mats in ((NEXP, (ones, tri0[:, 0:P])), (2 * NEXP, (ones, ones))):
                    for t in range(TB):
                        mm = nc.tensor.matmul(lo[:, 1, at:at + NEXP], mats[t], sel[:, t, :], start=False,
                                              stop=(t == 1), skip_group_check=True)
                mm.then_inc(ranks_done, 1)
                turn0 = pe.snap(start + l + 1)
                gather(turn0)
                pe.wait_ge(plan_ready, l + 2)
                n = pe.value_load(n_i[0:1, bass.ds(l, 1)], min_val=NEXP, max_val=MOST)
                with pe.Fori(0, n) as j:
                    g = pe.snap(start + j)
                    turn = pe.snap(turn0 + j)
                    expert = pe.value_load(expert_i[0:1, bass.ds(l * ITEMS + j, 1)], min_val=0, max_val=NEXP - 1)
                    last = pe.value_load(last_i[0:1, bass.ds(l * ITEMS + j, 1)], min_val=0, max_val=1)
                    full = pe.snap(l * (16 * TURNS) + expert * 16 + 32)
                    pe.wait_ge(xg_ready, turn)
                    with pe.If(last > 0):
                        item(True, full, g, turn)
                    with pe.Else():
                        item(False, full, g, turn)

        @block.scalar
        def _(a):
            def root(out_ap, in_ap):
                return nc.scalar.activation(out_ap, in_ap, ACT.Sqrt)

            a.dma_start(h[:], x_v).then_inc(x_full, 16)
            a.wait_ge(const_full, 16 * CONST_LOADS)
            with a.Fori(0, DEPTH) as l:
                a.wait_ge(plan_ready, l + 1)
                start = a.value_load(start_i[0:1, bass.ds(l, 1)], min_val=0, max_val=MOST * DEPTH)
                for b in range(2):
                    a.wait_ge(turned, 12 * l + b + 1)
                    nc.scalar.copy(actT[:, 2 * b:2 * b + 2, :].rearrange("p k s -> p (k s)"), lo[:, b, :]
                                   ).then_inc(actT_ready, 1)
                a.wait_ge(forget_arg, l + 1)
                nc.scalar.activation(fg[:, 3], fg[:, 2], ACT.Exp).then_inc(forget_log, 1)
                a.wait_ge(forget_log, 2 * l + 1)
                nc.scalar.activation(fg[:, 4], fg[:, 3], ACT.Ln, bias=1.0).then_inc(forget_log, 1)
                for n in range(TB * ROPE_CH, TB * N_CH):
                    a.wait_ge(z_done, 12 * l + n + 1)
                    c, t = n // TB, n % TB
                    nc.scalar.copy(z[:, t, c * CH:(c + 1) * CH], acc[:, 2 + t, :]).then_inc(z_copied, 1)
                for p in range(PAIRS + 1):
                    if p == 0:
                        a.wait_ge(qkT_done, l * PAIRS + 1)
                        nc.scalar.copy(qkT[:, 0].rearrange("p a b -> p (a b)"), acc[:, 0, :]).then_inc(qkT_ready, 1)
                    if p + 1 < PAIRS:
                        a.wait_ge(qkT_done, l * PAIRS + p + 2)
                        nc.scalar.copy(qkT[:, (p + 1) % 2].rearrange("p a b -> p (a b)"), acc[:, 0, :]
                                       ).then_inc(qkT_ready, 1)
                    if p < PAIRS:
                        for i in range(2):
                            hd = 2 * p + i
                            a.wait_ge(masked_ready, l * HEADS + hd + 1)
                            if hd >= 4:
                                a.wait_ge(probsT_done, l * HEADS + hd - 3)
                            nc.scalar.activation(probs[:, hd % 4, 0:P], masked[:, i, 0:P], ACT.Exp,
                                                 bias=neg_max[:, hd % 4, 0:1], scale=1 / INV_SCALE,
                                                 accum_out=row_sum[:, hd % 4, 0:1])
                            nc.scalar.activation(probs[:, hd % 4, P:SKEYS], masked[:, i, P:SKEYS], ACT.Exp,
                                                 bias=neg_max[:, hd % 4, 1:2], scale=1 / INV_SCALE,
                                                 accum_out=row_sum[:, hd % 4, 1:2]).then_inc(exp_done, 1)
                    if p >= 1:
                        for i in range(2):
                            hd = 2 * (p - 1) + i
                            a.wait_ge(pv_done, l * HEADS + hd + 1)
                            a.wait_ge(inv_ready, l * HEADS + hd + 1)
                            for t in range(TB):
                                op = nc.scalar.mul(mixed[:, t, hd * HD:(hd + 1) * HD], acc[:, 1 + i, t * HD:(t + 1) * HD],
                                                   row_inv[:, i, t:t + 1])
                            op.then_inc(mixed_done, 1)
                a.wait_ge(mixed_done, (l + 1) * HEADS)
                for t in range(TB):
                    for gi, (c0, c1) in enumerate(((0, D_DIL), (D_DIL, D))):
                        nc.scalar.activation(probs[:].rearrange("p a b -> p (a b)")[:, 0:c1 - c0], mixed[:, t, c0:c1],
                                             ACT.Square, accum_out=ssq[:, t, gi:gi + 1]).then_inc(ssq_done, 1)
                        a.wait_ge(ssq_done, 4 * l + 2 * t + gi + 1)
                a.wait_ge(ms_ready, l + 1)
                root(rms[:, 1], rms[:, 0]).then_inc(rms_root, 1)
                a.wait_ge(rms_ready, l + 1)
                for gi, (c0, c1) in enumerate(((0, D_DIL), (D_DIL, D))):
                    nc.scalar.mul(mixed[:, 0, c0:c1], mixed[:, 0, c0:c1], rms[:, 2, 0, gi:gi + 1]).then_inc(normed, 1)
                for b in range(2):
                    a.wait_ge(turned, 12 * l + 4 + b + 1)
                    for k in (2 * b, 2 * b + 1):
                        op = nc.scalar.mul(actT[:, k, :], lo[:, b, (k % 2) * SEQ:(k % 2 + 1) * SEQ], gmix[:, k:k + 1])
                    op.then_inc(actT_ready, 1)
                a.wait_ge(var_ready, 2 * l + 1)
                root(lnt[:, 1], lnt[:, 0]).then_inc(ln_root, 1)
                for b in range(2):
                    a.wait_ge(turned, 12 * l + 8 + b + 1)
                    nc.scalar.copy(actT[:, 2 * b:2 * b + 2, :].rearrange("p k s -> p (k s)"), lo[:, b, :]
                                   ).then_inc(actT_ready, 1)
                a.wait_ge(shifted, l + 1)
                nc.scalar.activation(rt[:, 1], rt[:, 0], ACT.Exp).then_inc(router_exp, 1)
                a.wait_ge(plan_ready, l + 2)
                n = a.value_load(n_i[0:1, bass.ds(l, 1)], min_val=NEXP, max_val=MOST)
                with a.Fori(0, n) as j:
                    g = a.snap(start + j)
                    a.wait_ge(gate_done, g + 1)
                    nc.scalar.activation(silu, lo[:, 0, :], ACT.Silu).then_inc(silu_done, 1)
                    a.wait_ge(act_turned, g + 1)
                    nc.scalar.copy(act_t.rearrange("p b half s -> p (b half s)"), lo[:, 1, :]
                                   ).then_inc(act_t_ready, 1)
                a.wait_ge(var_ready, 2 * l + 2)
                root(lnt[:, 1], lnt[:, 0]).then_inc(ln_root, 1)

        @block.vector
        def _(v):
            DVE_STEPS = 73
            steps = [0]
            base = [0]

            def step(ins):
                steps[0] += 1
                ins.then_inc(dve_step, 1)
                v.wait_ge(dve_step, base[0] + steps[0])

            def layer_norm(l, which):
                for t in range(TB):
                    for half in range(2):
                        op = nc.vector.bn_stats(stats[:, t, half, :], acc[:, 2 * t + half, :])
                step(op)
                v.sem_inc(passed, 1)
                for t in range(TB):
                    op = nc.vector.bn_aggr(mv[:, t, :], stats[:, t].rearrange("p a b -> p (a b)"))
                step(op)
                nc.vector.tensor_scalar(lnt[:, 0], mv[:, :, 1], LN_EPS, None, ALU.add).then_inc(var_ready, 1)
                v.wait_ge(ln_full, 64 * l + 32 * (which + 1))
                for t in range(TB):
                    op = nc.vector.scalar_tensor_tensor(out=h[:, t, :], in0=acc_tok[:, t, :], scalar=mv[:, t, 0:1],
                                                        in1=ln_gb[:, 0, :], op0=ALU.subtract, op1=ALU.mult)
                v.wait_ge(ln_root, 2 * l + which + 1)
                step(nc.vector.reciprocal(lnt[:, 2], lnt[:, 1]))
                for t in range(TB):
                    op = nc.vector.scalar_tensor_tensor(out=h[:, t, :], in0=h[:, t, :], scalar=lnt[:, 2, t:t + 1],
                                                        in1=ln_gb[:, 1, :], op0=ALU.mult, op1=ALU.add)
                op.then_inc(h_ready, 1)

            def ranks(dst, src, n):
                vals = src.rearrange("p (n i) -> p n i", i=4)
                vj = vals.unsqueeze(2).to_broadcast([P, n, 4, 4])
                vi = vals.unsqueeze(3).to_broadcast([P, n, 4, 4])
                ca, cb = (cmp[:, i, 0:16 * n] for i in range(2))
                nc.vector.tensor_tensor(ca.rearrange("p (n i j) -> p n i j", i=4, j=4), vj, vi, ALU.is_gt)
                step(nc.vector.tensor_tensor(cb.rearrange("p (n i j) -> p n i j", i=4, j=4), vj, vi, ALU.is_ge))
                nc.vector.tensor_tensor(ca, ca, cst[:, C_UP:C_UP + 16 * n], ALU.mult)
                step(nc.vector.tensor_tensor(cb, cb, cst[:, C_LO:C_LO + 16 * n], ALU.mult))
                step(nc.vector.tensor_tensor(ca, ca, cb, ALU.add))
                step(nc.vector.tensor_reduce(dst, ca.rearrange("p (n j) -> p n j", j=4), AX.X, ALU.add))

            def place_tokens(expert, block):
                for t in range(TB):
                    op = nc.vector.tensor_scalar(
                        place_t[:, t], iota[:, bass.ds(block * W, W)].unsqueeze(1).to_broadcast([P, 2, W]),
                        rank_tab[:, t, bass.ds(expert, 1)], None, ALU.is_equal)
                op.then_inc(place_ready, 1)

            def place_gates(expert, block):
                for t in range(TB):
                    nc.vector.tensor_scalar(
                        place_tg[:, t], iota[:, bass.ds(block * W, W)].unsqueeze(1).to_broadcast([P, 2, W]),
                        rank_tab[:, t, bass.ds(expert, 1)], gate_tab[:, t, bass.ds(expert, 1)],
                        ALU.is_equal, ALU.mult)

            def copy_gathered():
                for b in range(2):
                    op = nc.vector.tensor_copy(
                        xg[:, 4 * b:4 * b + 4, :],
                        lo[:, 2 + b, :].rearrange("p (k two s) -> p k two s", k=4, two=2)[:, :, 0, :])
                op.then_inc(xg_ready, 1)

            nc.vector.memset(startf[:], 0.0)
            nc.vector.memset(start_i[:], 0)
            nc.vector.memset(itab[:], 0.0).then_inc(plan_ready, 1)
            v.wait_ge(const_full, 16 * CONST_LOADS)
            v.wait_ge(x_full, 16)
            nc.vector.memset(nsub[:], 0.0).then_inc(h_ready, 1)
            with v.Fori(0, DEPTH) as l:
                base[0] = v.snap(l * DVE_STEPS)
                v.wait_ge(plan_ready, l + 1)
                start = v.value_load(start_i[0:1, bass.ds(l, 1)], min_val=0, max_val=MOST * DEPTH)
                for b in range(2, 4):
                    v.wait_ge(turned, 12 * l + b + 1)
                    nc.vector.tensor_copy(actT[:, 2 * b:2 * b + 2, :].rearrange("p k s -> p (k s)"), lo[:, b, :]
                                          ).then_inc(actT_ready, 1)
                v.wait_ge(forget_z, l + 1)
                step(nc.vector.tensor_tensor(fg[:, 0], acc[:, 1, 0:TB * N_FOX].rearrange("p (t n) -> p t n", t=TB),
                                             bf[:].to_broadcast([P, TB, N_FOX]), ALU.add))
                nc.vector.tensor_scalar(fg[:, 1], fg[:, 0], -1.0, 0.0, ALU.mult, ALU.max)
                nc.vector.scalar_tensor_tensor(out=fg[:, 2], in0=fg[:, 0], scalar=-1.0, in1=fg[:, 0], op0=ALU.mult,
                                               op1=ALU.min).then_inc(forget_arg, 1)
                for n in range(TB * ROPE_CH):
                    c, t = n // TB, n % TB
                    src = acc[:, 2 + t, :].rearrange("p (h two i) -> p h two i", two=2, i=32)
                    dst = z[:, t, c * CH:(c + 1) * CH].rearrange("p (h two i) -> p h two i", two=2, i=32)
                    cos, sin = (cst[:, C_COS + t * 64 + i * 32:C_COS + t * 64 + (i + 1) * 32].unsqueeze(1)
                                .to_broadcast([P, 8, 32]) for i in range(2))
                    t2sin = cmp[:, 0, :].rearrange("p (h i) -> p h i", i=32)
                    t1sin = cmp[:, 1, :].rearrange("p (h i) -> p h i", i=32)
                    v.wait_ge(z_done, 12 * l + n + 1)
                    nc.vector.tensor_tensor(dst[:, :, 0], src[:, :, 0], cos, ALU.mult)
                    nc.vector.tensor_tensor(t2sin, src[:, :, 1], sin, ALU.mult)
                    nc.vector.tensor_tensor(dst[:, :, 1], src[:, :, 1], cos, ALU.mult)
                    ins = nc.vector.tensor_tensor(t1sin, src[:, :, 0], sin, ALU.mult)
                    ins.then_inc(z_rope, 1)
                    v.wait_ge(z_rope, l * TB * ROPE_CH + n + 1)
                    nc.vector.tensor_tensor(dst[:, :, 0], dst[:, :, 0], t2sin, ALU.subtract)
                    nc.vector.tensor_tensor(dst[:, :, 1], dst[:, :, 1], t1sin, ALU.add).then_inc(z_rotated, 1)
                    v.wait_ge(z_rotated, l * TB * ROPE_CH + n + 1)
                v.wait_ge(forget_log, 2 * l + 2)
                step(nc.vector.tensor_tensor(fg[:, 6], fg[:, 1], fg[:, 4], ALU.add))
                step(nc.vector.tensor_scalar(fg[:, 5], fg[:, 6], INV_SCALE, None, ALU.mult))
                for t in range(TB):
                    for f in range(N_FOX):
                        op = nc.vector.tensor_scalar(decay[:, t, f, :], ones, fg[:, 5, t, f:f + 1], None, ALU.mult)
                op.then_inc(decay_ready, 1)
                v.wait_ge(cum_done, l + 1)
                step(nc.vector.tensor_copy(fg[:, 0].rearrange("p t n -> p (t n)"), acc[:, 1, 0:TB * N_FOX]))
                for p in range(PAIRS + 1):
                    if p < PAIRS:
                        for i in range(2):
                            hd = 2 * p + i
                            v.wait_ge(scores_done, l * HEADS + hd + 1)
                            if hd >= 2:
                                v.wait_ge(exp_done, l * HEADS + hd - 1)
                            if hd < N_DIL:
                                op = nc.vector.tensor_tensor(masked[:, i, :], lo[:, i, 0:SKEYS],
                                                             cst[:, C_MDIL:C_MDIL + SKEYS], ALU.add)
                            else:
                                f = hd - N_DIL
                                for t, (c0, c1) in enumerate(((0, P), (P, SKEYS))):
                                    op = nc.vector.scalar_tensor_tensor(
                                        out=masked[:, i, c0:c1], in0=lo[:, i, c0:c1], scalar=fg[:, 0, t, f:f + 1],
                                        in1=cst[:, C_MFOX + c0:C_MFOX + c1], op0=ALU.subtract, op1=ALU.add)
                            step(op)
                            nc.vector.tensor_reduce(row_max[:, i, 0:1], masked[:, i, 0:P], AX.X, ALU.max)
                            step(nc.vector.tensor_reduce(row_max[:, i, 1:2], masked[:, i, P:SKEYS], AX.X, ALU.max))
                            nc.vector.tensor_scalar(neg_max[:, hd % 4, :], row_max[:, i, :], -1 / INV_SCALE, None,
                                                    ALU.mult).then_inc(masked_ready, 1)
                    if p >= 1:
                        for i in range(2):
                            hd = 2 * (p - 1) + i
                            v.wait_ge(probsT_done, l * HEADS + hd + 1)
                            nc.vector.tensor_copy(probsT[:, i, :], lo[:, 2 + i, 0:SKEYS]).then_inc(probsT_ready, 1)
                            if hd >= 2:
                                v.wait_ge(mixed_done, l * HEADS + hd - 1)
                            nc.vector.reciprocal(row_inv[:, i, :], row_sum[:, hd % 4, :]).then_inc(inv_ready, 1)
                v.wait_ge(ssq_done, 4 * l + 4)
                nc.vector.tensor_scalar(rms[:, 0, :, 0], ssq[:, :, 0], 1.0 / D_DIL, RMS_EPS, ALU.mult, ALU.add)
                nc.vector.tensor_scalar(rms[:, 0, :, 1], ssq[:, :, 1], 1.0 / D_FOX, RMS_EPS, ALU.mult, ALU.add
                                        ).then_inc(ms_ready, 1)
                v.wait_ge(rms_root, l + 1)
                nc.vector.reciprocal(rms[:, 2], rms[:, 1]).then_inc(rms_ready, 1)
                v.wait_ge(rms_ready, l + 1)
                for gi, (c0, c1) in enumerate(((0, D_DIL), (D_DIL, D))):
                    nc.vector.tensor_scalar(mixed[:, 1, c0:c1], mixed[:, 1, c0:c1], rms[:, 2, 1, gi:gi + 1], None,
                                            ALU.mult).then_inc(normed, 1)
                for b in range(2, 4):
                    v.wait_ge(turned, 12 * l + 4 + b + 1)
                    for k in (2 * b, 2 * b + 1):
                        op = nc.vector.tensor_scalar(actT[:, k, :], lo[:, b, (k % 2) * SEQ:(k % 2 + 1) * SEQ],
                                                     gmix[:, k:k + 1], None, ALU.mult)
                    op.then_inc(actT_ready, 1)
                v.wait_ge(proj_done, l + 2)
                layer_norm(l, 0)
                for b in range(2, 4):
                    v.wait_ge(turned, 12 * l + 8 + b + 1)
                    nc.vector.tensor_copy(actT[:, 2 * b:2 * b + 2, :].rearrange("p k s -> p (k s)"), lo[:, b, :]
                                          ).then_inc(actT_ready, 1)
                v.wait_ge(logits_done, l + 1)
                step(nc.vector.tensor_tensor(rt[:, 2], lo[:, 0, 0:TB * NEXP].rearrange("p (t e) -> p t e", t=TB),
                                             br[:].to_broadcast([P, TB, NEXP]), ALU.add))
                step(nc.vector.tensor_reduce(r2[:, 0], rt[:, 2], AX.X, ALU.max))
                nc.vector.tensor_tensor(rt[:, 0], rt[:, 2], r2[:, 0].unsqueeze(2).to_broadcast([P, TB, NEXP]),
                                        ALU.subtract).then_inc(shifted, 1)
                v.wait_ge(router_exp, l + 1)
                step(nc.vector.tensor_reduce(r2[:, 1], rt[:, 1], AX.X, ALU.add))
                step(nc.vector.reciprocal(r2[:, 2], r2[:, 1]))
                step(nc.vector.tensor_tensor(rt[:, 2], rt[:, 1], r2[:, 2].unsqueeze(2).to_broadcast([P, TB, NEXP]),
                                             ALU.mult))
                probs16 = rt[:, 2].rearrange("p t e -> p (t e)")
                in_grp = rt[:, 3].rearrange("p t e -> p (t e)")
                ranks(in_grp, probs16, 8)
                best = rt[:, 4].rearrange("p t e -> p (t e)")
                step(nc.vector.scalar_tensor_tensor(out=best, in0=in_grp, scalar=1.5, in1=probs16, op0=ALU.is_lt,
                                                    op1=ALU.mult))
                step(nc.vector.tensor_reduce(r8[:, 0], best.rearrange("p (g i) -> p g i", i=4), AX.X, ALU.add))
                ranks(r8[:, 1], r8[:, 0], 2)
                step(nc.vector.tensor_scalar(r8[:, 2], r8[:, 1], 0.5, None, ALU.is_lt))
                chosen = r8[:, 2].unsqueeze(2).to_broadcast([P, 8, 4])
                nc.vector.scalar_tensor_tensor(out=sel[:].rearrange("p t (g i) -> p (t g) i", i=4),
                                               in0=in_grp.rearrange("p (g i) -> p g i", i=4), scalar=1.5, in1=chosen,
                                               op0=ALU.is_lt, op1=ALU.mult).then_inc(sel_ready, 1)
                step(nc.vector.tensor_tensor(rt[:, 5].rearrange("p t (g i) -> p (t g) i", i=4),
                                             best.rearrange("p (g i) -> p g i", i=4), chosen, ALU.mult))
                step(nc.vector.tensor_reduce(r2[:, 3], rt[:, 5], AX.X, ALU.add))
                step(nc.vector.reciprocal(r2[:, 4], r2[:, 3]))
                nc.vector.tensor_tensor(gate_tab[:], rt[:, 5],
                                        r2[:, 4].unsqueeze(2).to_broadcast([P, TB, NEXP]), ALU.mult)
                v.wait_ge(ranks_done, l + 1)
                step(nc.vector.tensor_tensor(rank_tab[:],
                                             lo[:, 1, 0:TB * NEXP].rearrange("p (t e) -> p t e", t=TB), sel[:],
                                             ALU.mult))
                turn0 = v.snap(start + l + 1)
                place_tokens(0, 0)
                count = lo[:, 1, 2 * NEXP:3 * NEXP]
                step(nc.vector.tensor_scalar(nsub[:, 0], count, W + 0.5, 1.0, ALU.is_gt, ALU.add))
                for c in range(2, SEQ // W):
                    step(nc.vector.scalar_tensor_tensor(out=nsub[:, 0], in0=count, scalar=W * c + 0.5,
                                                        in1=nsub[:, 0], op0=ALU.is_gt, op1=ALU.add))
                upto = pscratch[:, 0:NEXP * NEXP].rearrange("p (e f) -> p e f", e=NEXP)
                step(nc.vector.tensor_tensor(upto, cst[:, C_L16:C_L16 + 256].rearrange("p (e f) -> p e f", e=NEXP),
                                             nsub[:, 0].unsqueeze(1).to_broadcast([P, NEXP, NEXP]), ALU.mult))
                step(nc.vector.tensor_reduce(nsub[:, 1], upto, AX.X, ALU.add))
                ended, ends = (pscratch[:, c:c + ITEMS * NEXP].rearrange("p (i e) -> p i e", i=ITEMS)
                               for c in (256, 768))
                cum = nsub[:, 1].unsqueeze(1).to_broadcast([P, ITEMS, NEXP])
                count_i = iota[:, 0:ITEMS].unsqueeze(2).to_broadcast([P, ITEMS, NEXP])
                nc.vector.tensor_tensor(ends, cum, count_i, ALU.is_equal)
                step(nc.vector.tensor_tensor(ended, cum, count_i, ALU.is_lt))
                nc.vector.tensor_reduce(itab[:, 2], ends, AX.X, ALU.add)
                step(nc.vector.tensor_reduce(itab[:, 0], ended, AX.X, ALU.add))
                step(nc.vector.tensor_tensor(ended, ended, nsub[:, 0].unsqueeze(1).to_broadcast([P, ITEMS, NEXP]),
                                             ALU.mult))
                step(nc.vector.tensor_reduce(itab[:, 1], ended, AX.X, ALU.add))
                step(nc.vector.scalar_tensor_tensor(out=itab[:, 3], in0=itab[:, 1], scalar=-1.0,
                                                    in1=iota[:, 0:ITEMS], op0=ALU.mult, op1=ALU.add))
                own = l * ITEMS
                nc.vector.tensor_scalar(expert_i[:, bass.ds(own, ITEMS)], itab[:, 0], NEXP - 1.0, None, ALU.min)
                nc.vector.tensor_scalar(block_i[:, bass.ds(own, ITEMS)], itab[:, 3], -1.0, 0.0, ALU.add, ALU.max)
                nc.vector.tensor_copy(last_i[:, bass.ds(own, ITEMS)], itab[:, 2])
                nc.vector.tensor_copy(n_i[:, bass.ds(l, 1)], nsub[:, 1, NEXP - 1:NEXP])
                step(nc.vector.tensor_tensor(startf[:, bass.ds(l + 1, 1)], startf[:, bass.ds(l, 1)],
                                             nsub[:, 1, NEXP - 1:NEXP], ALU.add))
                nc.vector.tensor_copy(start_i[:, bass.ds(l + 1, 1)], startf[:, bass.ds(l + 1, 1)]
                                      ).then_inc(plan_ready, 1)
                v.wait_ge(gathered, turn0)
                copy_gathered()
                v.wait_ge(plan_ready, l + 2)
                v.sem_inc(passed, 1)
                n = v.value_load(n_i[0:1, bass.ds(l, 1)], min_val=NEXP, max_val=MOST)
                with v.Fori(0, n) as j:
                    g = v.snap(start + j)
                    turn = v.snap(turn0 + j)
                    at = v.snap(l * ITEMS + j)
                    place_gates(v.value_load(expert_i[0:1, bass.ds(at, 1)], min_val=0, max_val=NEXP - 1),
                                v.value_load(block_i[0:1, bass.ds(at, 1)], min_val=0, max_val=SEQ // W - 1))
                    place_tokens(v.value_load(expert_i[0:1, bass.ds(at + 1, 1)], min_val=0, max_val=NEXP - 1),
                                 v.value_load(block_i[0:1, bass.ds(at + 1, 1)], min_val=0, max_val=SEQ // W - 1))
                    v.wait_ge(up_done, g + 1)
                    v.wait_ge(silu_done, g + 1)
                    nc.vector.tensor_tensor(act, lo[:, 1, :], silu, ALU.mult).then_inc(act_ready, 1)
                    v.wait_ge(gathered, turn + 1)
                    copy_gathered()
                    v.wait_ge(placeT_done, g + 1)
                    nc.vector.tensor_copy(place_gt, lo[:, 2, 0:SEQ]).then_inc(placeT_ready, 1)
                    v.wait_ge(down_done, g + 1)
                    nc.vector.tensor_copy(y, lo[:, 0, :]).then_inc(y_ready, 1)
                v.wait_ge(scattered, start + n)
                layer_norm(l, 1)
            assert steps[0] == DVE_STEPS, steps[0]


_INS = ['x', 'w_in', 'b_forget', 'g_dil', 'g_fox', 'w_out', 'ln1_g', 'ln1_b', 'w_router', 'b_router',
        'w_gate', 'w_up', 'w_down', 'ln2_g', 'ln2_b']


def kernel(**inputs):
    import numpy as _np
    import concourse.bacc as _bacc
    from concourse import mybir as _mybir
    from concourse.bass_utils import run_bass_kernel_spmd as _run

    nc = _bacc.Bacc("TRN2", target_bir_lowering=False, num_devices=1, dynamic_dma_scratch_size=8192)
    arrays, args = {}, []
    for name in _INS + ['consts']:
        a = constants() if name == 'consts' else _np.ascontiguousarray(inputs[name])
        arrays[f"in_{name}_dram"] = a
        args.append(nc.dram_tensor(f"in_{name}_dram", a.shape, _mybir.dt.from_np(a.dtype), kind="ExternalInput").ap())
    args.append(nc.dram_tensor("out_dram", (1, SEQ, D), F32, kind="ExternalOutput").ap())
    build(nc, *args)
    r = _run(nc, [arrays], core_ids=[0])
    return r.results[0]["out_dram"]
```

```python
from contextlib import ExitStack

import numpy as np

import concourse.bass as bass
from concourse import mybir

ALU = mybir.AluOpType
ACT = mybir.ActivationFunctionType
AX = mybir.AxisListType
F32 = mybir.dt.float32
I32 = mybir.dt.int32

P = 128
DEPTH, SEQ, D = 2, 256, 1024
HD = 64
N_DIL, N_FOX = 12, 4
HEADS = N_DIL + N_FOX
PAIRS = HEADS // 2
D_DIL, D_FOX = N_DIL * HD, N_FOX * HD
Q_DIL, K_DIL, V_DIL = 0, D_DIL, 2 * D_DIL
Q_FOX = 3 * D_DIL
K_FOX, V_FOX = Q_FOX + D_FOX, Q_FOX + 2 * D_FOX
ZF = V_FOX + D_FOX
TB = SEQ // P
KB = D // P
CH = 512
N_CH = ZF // CH
ROPE_CH = 2 * D_DIL // CH
NEXP, NGRP, EPG = 16, 4, 4
W = 64
MOST = NEXP + (2 * SEQ - 1) // (P + 1)
ITEMS = MOST + 1
SLOTS = 16
EVEN, UP, DOWN, ODD = 0, 4, 8, 12
TURNS = NEXP + 1
GATE_TURNS = NEXP // 2 + 1
ALPHA = (2.0 * DEPTH) ** 0.25
LN_EPS, RMS_EPS = 1e-5, 1e-6
INV_SCALE = 8.0
NEG = -1e30
SKEYS = P + SEQ

C_ID, C_AID = 0, P
C_TRI0, C_TRI1 = 2 * P, 2 * P + SEQ
C_MDIL = C_TRI1 + SEQ
C_MFOX = C_MDIL + SKEYS
C_COS = C_MFOX + SKEYS
C_IOTA = C_COS + TB * 2 * 32
C_PLACES = C_IOTA + SEQ
C_UP = C_PLACES + 3 * P
C_LO = C_UP + 8 * 16
C_L16 = C_LO + 8 * 16
C_ODD = C_L16 + NEXP * NEXP
C_END = C_ODD + NEXP


def constants():
    t = np.zeros((P, C_END), np.float32)
    p = np.arange(P)
    t[:, C_ID:C_ID + P] = np.eye(P)
    t[:, C_AID:C_AID + P] = np.eye(P) * ALPHA
    j = np.arange(SEQ)
    t[:, C_TRI0:C_TRI0 + SEQ] = p[:, None] <= j[None]
    t[:, C_TRI1:C_TRI1 + SEQ] = p[:, None] + P <= j[None]
    for b in range(TB):
        keys = np.arange(P * (b + 1))
        delta = (p[:, None] + b * P) - keys[None]
        ok = delta >= 0
        n = (ok & (delta <= 128)) * 1.0 + (ok & (delta % 4 == 0)) + (ok & (delta % 16 == 0))
        at = b * P
        bias = np.where(n > 0, INV_SCALE * np.log(np.maximum(n, 1)), NEG)
        t[:, C_MDIL + at:C_MDIL + at + len(keys)] = bias
        t[:, C_MFOX + at:C_MFOX + at + len(keys)] = np.where(ok, 0.0, NEG)
        inv = (np.float32(10000.0) ** (-np.arange(32, dtype=np.float32) / np.float32(32))).astype(np.float32)
        ang = ((p + b * P).astype(np.float32)[:, None] * inv[None]).astype(np.float32)
        t[:, C_COS + b * 64:C_COS + b * 64 + 32] = np.cos(ang)
        t[:, C_COS + b * 64 + 32:C_COS + b * 64 + 64] = np.sin(ang)
    t[:, C_IOTA:C_IOTA + SEQ] = np.arange(1, SEQ + 1)
    t[:, C_PLACES:C_PLACES + P] = np.arange(P) % W + 1
    t[:, C_PLACES + P:C_PLACES + 3 * P] = np.arange(1, SEQ + 1)
    i4 = np.arange(4)
    t[:, C_UP:C_UP + 128] = np.tile((i4[None] > i4[:, None]).astype(np.float32).ravel(), 8)
    t[:, C_LO:C_LO + 128] = np.tile((i4[None] < i4[:, None]).astype(np.float32).ravel(), 8)
    e = np.arange(NEXP)
    t[:, C_L16:C_L16 + 256] = (e[None] <= e[:, None]).astype(np.float32).ravel()
    t[:, C_ODD:C_END] = e % 2
    return t


def head_cols(h):
    if h < N_DIL:
        return Q_DIL + h * HD, K_DIL + h * HD, V_DIL + h * HD
    return Q_FOX + (h - N_DIL) * HD, K_FOX + (h - N_DIL) * HD, V_FOX + (h - N_DIL) * HD


def build(nc, x, w_in, b_forget, g_dil, g_fox, w_out, ln1_g, ln1_b, w_router, b_router,
          w_gate, w_up, w_down, ln2_g, ln2_b, consts, out):
    with ExitStack() as ctx:
        def sb(name, shape, dt=F32):
            return ctx.enter_context(nc.sbuf_tensor(name, shape, dt))

        def sem(name):
            return ctx.enter_context(nc.semaphore(name))

        ring = sb("ring", [P, SLOTS, 2048])
        wout = ring[:, ODD:ODD + 4, :].rearrange("p s (k n) -> p (s k) n", n=D)
        cst = sb("cst", [P, C_END])
        h = sb("h", [P, TB, D])
        actT = sb("actT", [P, KB, SEQ])
        z = sb("z", [P, TB, ZF])
        qkT = sb("qkT", [P, 2, 4, P])
        masked = sb("masked", [P, 2, SKEYS])
        probs = sb("probs", [P, 4, SKEYS])
        probsT = sb("probsT", [P, 2, SKEYS])
        decay = sb("decay", [P, TB, N_FOX, P])
        ln_gb = sb("ln_gb", [P, 2, D])
        wf = sb("wf", [P, KB, N_FOX])
        bf = sb("bf", [P, 1, N_FOX])
        gmix = sb("gmix", [P, KB])
        wr = sb("wr", [P, KB, NEXP])
        br = sb("br", [P, 1, NEXP])
        fg = sb("fg", [P, 7, TB, N_FOX])
        row_max = sb("row_max", [P, 2, TB])
        neg_max = sb("neg_max", [P, 4, TB])
        row_sum = sb("row_sum", [P, 4, TB])
        row_inv = sb("row_inv", [P, 2, TB])
        ssq = sb("ssq", [P, TB, 2])
        rms = sb("rms", [P, 3, TB, 2])
        stats = sb("stats", [P, TB, 2, 6])
        mv = sb("mv", [P, TB, 2])
        lnt = sb("lnt", [P, 3, TB])
        rt = sb("rt", [P, 6, TB, NEXP])
        r8 = sb("r8", [P, 6, 8])
        r2 = sb("r2", [P, 5, TB])
        cmp = probs[:].rearrange("p a b -> p (a b)")[:, 0:512].rearrange("p (a b) -> p a b", a=2)
        sel = sb("sel", [P, TB, NEXP])
        rank_tab = sb("rank_tab", [P, TB, NEXP])
        gate_tab = sb("gate_tab", [P, TB, NEXP])
        nsub = sb("nsub", [P, 2, NEXP])
        wide_shift = sb("wide_shift", [P, 1])
        wide = sb("wide", [P, NEXP + 1])
        kind_step = sb("kind_step", [P, 2, NEXP])
        itab = sb("itab", [P, 4, ITEMS])
        startf = sb("startf", [P, DEPTH + 1])
        start_i = sb("start_i", [P, DEPTH + 1], I32)
        n_i = sb("n_i", [P, DEPTH], I32)
        expert_i = sb("expert_i", [P, DEPTH * ITEMS], I32)
        kind_i = sb("kind_i", [P, DEPTH * ITEMS], I32)
        odd_i = sb("odd_i", [P, NEXP], I32)
        last_i = sb("last_i", [P, DEPTH * ITEMS], I32)

        zflat = z[:].rearrange("p t c -> p (t c)")
        xg = zflat[:, 0:1024].rearrange("p (k s) -> p k s", k=KB)
        silu = zflat[:, 1024:2048]
        act = zflat[:, 2048:3072]
        act_t = zflat[:, 3072:4096]
        y = zflat[:, 4096:5120]
        place_gt = zflat[:, 5120:5376]
        place_tg = zflat[:, 5376:5632].rearrange("p (t s) -> p t s", t=TB)
        place_t = zflat[:, 5632:5888].rearrange("p (t s) -> p t s", t=TB)
        mixed = z[:, :, 0:D]

        lo = ctx.enter_context(nc.psum_tensor("lo", [P, 4, 512], F32))
        acc = ctx.enter_context(nc.psum_tensor("acc", [P, 4, 512], F32))
        lo_flat = lo[:].rearrange("p b c -> p (b c)")
        acc_tok = acc[:].rearrange("p (t b) c -> p t (b c)", t=TB)

        ident = cst[:, C_ID:C_ID + P]
        alpha_ident = cst[:, C_AID:C_AID + P]
        tri0 = cst[:, C_TRI0:C_TRI0 + SEQ]
        tri1 = cst[:, C_TRI1:C_TRI1 + SEQ]
        ones = cst[:, C_TRI0 + P:C_TRI0 + 2 * P]
        iota = cst[:, C_IOTA:C_IOTA + SEQ]
        places = cst[:, C_PLACES:C_PLACES + 3 * P]
        squares = decay[:].rearrange("p t n q -> p (t n q)")
        pscratch = probs[:].rearrange("p a b -> p (a b)")

        x_full, ident_full, const_full = sem("x_full"), sem("ident_full"), sem("const_full")
        ring_full = [sem(f"ring_full{i}") for i in range(SLOTS)]
        small_full, ln_full, out_full = sem("small_full"), sem("ln_full"), sem("out_full")
        ring_free = [sem(f"ring_free{i}") for i in range(SLOTS)]
        h_ready = sem("h_ready")
        turned = sem("turned")
        actT_act = sem("actT_act")
        actT_dve = sem("actT_dve")
        forget_z = sem("forget_z")
        forget_arg = sem("forget_arg")
        forget_log = sem("forget_log")
        decay_ready = sem("decay_ready")
        cum_done = sem("cum_done")
        cum_read = sem("cum_read")
        z_done = sem("z_done")
        z_rope = sem("z_rope")
        z_copied = sem("z_copied")
        z_rotated = sem("z_rotated")
        qkT_done = sem("qkT_done")
        qkT_ready = sem("qkT_ready")
        scores_done = sem("scores_done")
        masked_ready = sem("masked_ready")
        exp_done = sem("exp_done")
        probsT_done = sem("probsT_done")
        probsT_ready = sem("probsT_ready")
        inv_ready = sem("inv_ready")
        pv_done = sem("pv_done")
        mixed_done = sem("mixed_done")
        ssq_done = sem("ssq_done")
        ms_ready = sem("ms_ready")
        rms_root = sem("rms_root")
        rms_ready = sem("rms_ready")
        normed0 = sem("normed0")
        normed1 = sem("normed1")
        proj_done = sem("proj_done")
        var_ready = sem("var_ready")
        ln_root = sem("ln_root")
        logits_done = sem("logits_done")
        shifted = sem("shifted")
        router_exp = sem("router_exp")
        sel_ready = sem("sel_ready")
        ranks_done = sem("ranks_done")
        plan_ready = sem("plan_ready")
        dve_step = sem("dve_step")
        place_ready, gathered, xg_ready = sem("place_ready"), sem("gathered"), sem("xg_ready")
        gate_done, up_done, silu_done, act_ready = sem("gate_done"), sem("up_done"), sem("silu_done"), sem("act_ready")
        act_turned, act_t_ready = sem("act_turned"), sem("act_t_ready")
        placeT_done, placeT_ready = sem("placeT_done"), sem("placeT_ready")
        down_done, y_ready, scattered = sem("down_done"), sem("y_ready"), sem("scattered")

        passed = sem("passed")

        x_v = x.rearrange("b (t p) d -> p (b t) d", p=P)
        out_v = out.rearrange("b (t p) d -> p (b t) d", p=P)
        w_in_v = w_in.rearrange("l (k p) n -> p l k n", p=P)
        w_out_v = w_out.rearrange("l (k p) n -> p l k n", p=P)
        wr_v = w_router.rearrange("(k p) e -> p k e", p=P)
        expert_v = [w.rearrange("l e (k p) f -> p l e k f", p=P) for w in (w_gate, w_up, w_down)]
        CONST_LOADS = 3
        SMALL = 4 * 16

        block = ctx.enter_context(nc.Block())

        @block.sync
        def _(sp):
            for s in range(SLOTS):
                sp.sem_inc(ring_free[s], 1)
            sp.sem_inc(proj_done, 1)

            def load_small(layer):
                with nc.allow_non_contiguous_dma(reason="small vectors laid over the partitions"):
                    sp.dma_start(wf[:], w_in_v[:, bass.ds(layer, 1), :, ZF:ZF + N_FOX].rearrange("p l k n -> p (l k) n")
                                 ).then_inc(small_full, 16)
                    sp.dma_start(bf[:, 0, :], b_forget[bass.ds(layer, 1)].rearrange("l n -> (l n)").partition_broadcast(P)
                                 ).then_inc(small_full, 16)
                    sp.dma_start(gmix[:, 0:D_DIL // P], g_dil[bass.ds(layer, 1)].rearrange("l (k p) -> p (l k)", p=P)
                                 ).then_inc(small_full, 16)
                    sp.dma_start(gmix[:, D_DIL // P:KB], g_fox[bass.ds(layer, 1)].rearrange("l (k p) -> p (l k)", p=P)
                                 ).then_inc(small_full, 16)

            sp.dma_start(cst[:, C_ID:C_ID + P], consts[:, C_ID:C_ID + P]).then_inc(ident_full, 16)
            sp.dma_start(h[:], x_v).then_inc(x_full, 16)

            def load_matrix(layer, m, expert, first, turn):
                for i in range(4):
                    s = first + i
                    sp.wait_ge(ring_free[s], turn)
                    src = expert_v[m][:, bass.ds(layer, 1), bass.ds(expert, 1), 2 * i:2 * i + 2, :]
                    sp.dma_start(ring[:, s, :], src.rearrange("p l e k f -> p (l e k) f")).then_inc(ring_full[s], 16)

            with sp.Fori(0, DEPTH) as l:
                turn = sp.snap(l * TURNS + 1)
                gate_turn = sp.snap(l * GATE_TURNS + 1)
                for c in range(N_CH):
                    if c == 1:
                        sp.wait_ge(proj_done, 2 * l + 1)
                        sp.sem_inc(passed, 1)
                        load_small(l)
                        with sp.If(l < 1):
                            sp.dma_start(cst[:, P:C_END], consts[:, P:C_END]).then_inc(const_full, 16)
                            sp.dma_start(wr[:], wr_v).then_inc(const_full, 16)
                            sp.dma_start(br[:, 0, :], b_router.partition_broadcast(P)).then_inc(const_full, 16)
                        sp.sem_inc(passed, 1)
                    for half in range(2):
                        s = 2 * c + half
                        sp.wait_ge(ring_free[s], gate_turn if s < UP else turn)
                        src = w_in_v[:, bass.ds(l, 1), 4 * half:4 * half + 4, c * CH:(c + 1) * CH]
                        sp.dma_start(ring[:, s, :].rearrange("p (k n) -> p k n", k=4),
                                     src.rearrange("p l k n -> p (l k) n")).then_inc(ring_full[s], 16)
                for q in range(4):
                    sp.wait_ge(ring_free[ODD + q], gate_turn)
                    src = w_out_v[:, bass.ds(l, 1), 2 * q:2 * q + 2, :]
                    sp.dma_start(wout[:, 2 * q:2 * q + 2, :],
                                 src.rearrange("p l k n -> p (l k) n")).then_inc(ring_full[ODD + q], 16)
                load_matrix(l, 0, 0, EVEN, sp.snap(gate_turn + 1))
                load_matrix(l, 1, 0, UP, sp.snap(turn + 1))
                load_matrix(l, 2, 0, DOWN, sp.snap(turn + 1))
                load_matrix(l, 0, 1, ODD, sp.snap(gate_turn + 1))
                with sp.Fori(0, NEXP // 2 - 1) as j:
                    for i, first in ((1, EVEN), (2, ODD)):
                        load_matrix(l, 0, sp.snap(2 * j + i + 1), first, sp.snap(gate_turn + j + 2))
                        load_matrix(l, 1, sp.snap(2 * j + i), UP, sp.snap(turn + 2 * j + i + 1))
                        load_matrix(l, 2, sp.snap(2 * j + i), DOWN, sp.snap(turn + 2 * j + i + 1))
                load_matrix(l, 1, NEXP - 1, UP, sp.snap(turn + NEXP))
                load_matrix(l, 2, NEXP - 1, DOWN, sp.snap(turn + NEXP))
            sp.wait_ge(h_ready, 2 + 4 * DEPTH)
            sp.dma_start(out_v, h[:]).then_inc(out_full, 16)
            sp.wait_ge(out_full, 16)

        @block.gpsimd
        def _(pool):
            def load_norm(layer, g, b):
                for i, v in enumerate((g, b)):
                    pool.dma_start(ln_gb[:, i, :], v[bass.ds(layer, 1)].rearrange("l d -> (l d)").partition_broadcast(P)
                                   ).then_inc(ln_full, 16)

            with pool.Fori(0, DEPTH) as l:
                pool.wait_ge(h_ready, 4 * l + 2)
                pool.sem_inc(passed, 1)
                load_norm(l, ln1_g, ln1_b)
                pool.wait_ge(h_ready, 4 * l + 4)
                pool.sem_inc(passed, 1)
                load_norm(l, ln2_g, ln2_b)

        @block.tensor
        def _(pe):
            def turn_block(src, t, release=None):
                for b in range(2):
                    for i in range(4):
                        k = 4 * b + i
                        mm = nc.tensor.transpose(lo[:, 2 * t + b, i * P:(i + 1) * P], src[:, t, k * P:(k + 1) * P],
                                                 ident)
                        if release is not None and k == 0:
                            mm.then_inc(release, 1)
                    mm.then_inc(turned, 1)

            def seed(t):
                for half in range(2):
                    nc.tensor.matmul(acc[:, 2 * t + half, :], alpha_ident, h[:, t, half * 512:(half + 1) * 512],
                                     start=True, stop=False, skip_group_check=True)

            def turn_qk(l, p, release=None):
                if p >= 1:
                    pe.wait_ge(qkT_ready, l * PAIRS + p)
                cols = head_cols(2 * p)
                for i in range(4):
                    mm = nc.tensor.transpose(acc[:, 0, i * P:(i + 1) * P],
                                             z[:, i % 2, cols[i // 2]:cols[i // 2] + P], ident)
                    if release is not None and i == 0:
                        mm.then_inc(release, 1)
                mm.then_inc(qkT_done, 1)

            def scores(l, p):
                pe.wait_ge(qkT_ready, l * PAIRS + p + 1)
                for i in range(2):
                    hd = 2 * p + i
                    if hd >= 2:
                        pe.wait_ge(masked_ready, l * HEADS + hd - 1)
                    r = slice(i * HD, (i + 1) * HD)
                    qk = qkT[r, p % 2]
                    fox = hd >= N_DIL
                    f = hd - N_DIL
                    mm = nc.tensor.matmul(lo[:, i, 0:P], qk[:, 0, :], qk[:, 2, :], start=True, stop=not fox,
                                          skip_group_check=True)
                    mm = nc.tensor.matmul(lo[:, i, P:SKEYS], qk[:, 1, :], qk[:, 2:4, :].rearrange("p a b -> p (a b)"),
                                          start=False, stop=not fox, skip_group_check=True)
                    if fox:
                        nc.tensor.matmul(lo[:, i, 0:P], decay[:, 0, f, :], tri0[:, 0:P], start=False, stop=False,
                                         skip_group_check=True)
                        nc.tensor.matmul(lo[:, i, P:SKEYS], decay[:, 0, f, :], tri0, start=False, stop=False,
                                         skip_group_check=True)
                        mm = nc.tensor.matmul(lo[:, i, 2 * P:SKEYS], decay[:, 1, f, :], tri1[:, P:SEQ], start=False,
                                              stop=True, skip_group_check=True)
                    mm.then_inc(scores_done, 1)

            def turn_probs(l, p):
                for i in range(2):
                    hd = 2 * p + i
                    pe.wait_ge(exp_done, l * HEADS + hd + 1)
                    if hd >= 2:
                        pe.wait_ge(probsT_ready, l * HEADS + hd - 1)
                    for b in range(3):
                        mm = nc.tensor.transpose(lo[:, 2 + i, b * P:(b + 1) * P],
                                                 probs[:, hd % 4, b * P:(b + 1) * P], ident)
                    mm.then_inc(probsT_done, 1)

            def weigh_values(l, p):
                for i in range(2):
                    hd = 2 * p + i
                    v = head_cols(hd)[2]
                    pe.wait_ge(probsT_ready, l * HEADS + hd + 1)
                    if hd >= 2 and i == 0:
                        pe.wait_ge(mixed_done, l * HEADS + hd)
                    at = i * 2 * HD
                    nc.tensor.matmul(acc[:, 1, at:at + HD], probsT[:, i, 0:P], z[:, 0, v:v + HD],
                                     start=True, stop=True, skip_group_check=True)
                    nc.tensor.matmul(acc[:, 1, at + HD:at + 2 * HD], probsT[:, i, P:2 * P], z[:, 0, v:v + HD],
                                     start=False, stop=False, skip_group_check=True)
                    nc.tensor.matmul(acc[:, 1, at + HD:at + 2 * HD], probsT[:, i, 2 * P:3 * P], z[:, 1, v:v + HD],
                                     start=False, stop=True, skip_group_check=True).then_inc(pv_done, 1)

            def gather(ks, release=None):
                for k in ks:
                    for t in range(TB):
                        mm = nc.tensor.matmul(lo[:, 2 + k // 4, (k % 4) * P:(k % 4 + 1) * P],
                                              h[:, t, k * P:(k + 1) * P], place_t[:, t],
                                              start=(k % 4 == 0 and t == 0), stop=(t == 1), skip_group_check=True)
                        if release is not None and k == ks[0] and t == 0:
                            mm.then_inc(release, 1)
                    if k % 4 == 3:
                        mm.then_inc(gathered, 1)

            def halves(bank, lhsT, s, kk, start, stop):
                for half in range(2):
                    at = kk * D + half * 512
                    mm = nc.tensor.matmul(lo[half * W:(half + 1) * W, bank, :], lhsT, ring[:, s, at:at + 512],
                                          start=start, stop=stop, skip_group_check=True)
                return mm

            def turn_gates():
                for t in range(TB):
                    mm = nc.tensor.transpose(lo[:, 3, t * P:(t + 1) * P], place_tg[:, t], ident)
                mm.then_inc(placeT_done, 1)

            def narrow_gate(first, gate_full, full):
                for i in range(4):
                    pe.wait_ge(ring_full[first + i], gate_full)
                    for kk in range(2):
                        k = 2 * i + kk
                        mm = halves(0, xg[:, k, 0:W], first + i, kk, k == 0, k == KB - 1)
                    mm.then_inc(gate_done if i == 3 else ring_free[first + i], 1)
                pe.wait_ge(ring_full[UP], full)
                halves(1, xg[:, 0, 0:W], UP, 0, True, False).then_inc(ring_free[first + 3], 1)

            def narrow_item(full, g, turn):
                for i in range(4):
                    if i >= 1:
                        pe.wait_ge(ring_full[UP + i], full)
                    for k in range(max(2 * i, 1), 2 * i + 2):
                        mm = halves(1, xg[:, k, 0:W], UP + i, k % 2, False, k == KB - 1)
                    mm.then_inc(up_done if i == 3 else ring_free[UP + i], 1)
                pe.wait_ge(place_ready, turn + 1)
                gather(range(3), ring_free[UP + 3])
                pe.wait_ge(act_ready, g + 1)
                for b in range(4):
                    mm = nc.tensor.transpose(lo[:, 1, b * P:(b + 1) * P], act[:, b * P:(b + 1) * P], ident)
                mm.then_inc(act_turned, 1)
                turn_gates()
                gather(range(3, 4))
                pe.wait_ge(act_t_ready, g + 1)
                for s in range(4):
                    pe.wait_ge(ring_full[DOWN + s], full)
                    for kk in range(2):
                        f = 2 * s + kk
                        at = (f % 4) * P + (f // 4) * W
                        mm = halves(0, act_t[:, at:at + W], DOWN + s, kk, f == 0, f == KB - 1)
                    mm.then_inc(down_done if s == 3 else ring_free[DOWN + s], 1)
                pe.wait_ge(placeT_ready, g + 1)
                gather(range(4, KB), ring_free[DOWN + 3])
                pe.wait_ge(y_ready, g + 1)
                for t in range(TB):
                    for half in range(2):
                        r = slice(half * W, (half + 1) * W)
                        mm = nc.tensor.matmul(acc[:, 2 * t + half, :], place_gt[r, t * P:(t + 1) * P], y[r, 0:512],
                                              start=False, stop=True, skip_group_check=True)
                mm.then_inc(scattered, 1)

            def wide_product(bank, lhsT, s, kk, start, stop):
                for half in range(2):
                    at = kk * D + half * 512
                    mm = nc.tensor.matmul(lo[:, bank + half, :], lhsT, ring[:, s, at:at + 512],
                                          start=start, stop=stop, skip_group_check=True)
                return mm

            def wide_gate(last, first, gate_full, full):
                for i in range(4):
                    pe.wait_ge(ring_full[first + i], gate_full)
                    for kk in range(2):
                        k = 2 * i + kk
                        mm = wide_product(0, xg[:, k, :], first + i, kk, k == 0, k == KB - 1)
                    if i == 3:
                        mm.then_inc(gate_done, 1)
                    elif last:
                        mm.then_inc(ring_free[first + i], 1)
                pe.wait_ge(ring_full[UP], full)
                mm = wide_product(2, xg[:, 0, :], UP, 0, True, False)
                if last:
                    mm.then_inc(ring_free[first + 3], 1)

            def wide_item(last, full, g, turn):
                for i in range(4):
                    if i >= 1:
                        pe.wait_ge(ring_full[UP + i], full)
                    for k in range(max(2 * i, 1), 2 * i + 2):
                        mm = wide_product(2, xg[:, k, :], UP + i, k % 2, False, k == KB - 1)
                    if i == 3:
                        mm.then_inc(up_done, 1)
                    elif last:
                        mm.then_inc(ring_free[UP + i], 1)
                pe.wait_ge(act_ready, g + 1)
                for b in range(KB):
                    mm = nc.tensor.transpose(lo[:, b // 4, (b % 4) * P:(b % 4 + 1) * P], act[:, b * P:(b + 1) * P],
                                             ident)
                    if last and b == 0:
                        mm.then_inc(ring_free[UP + 3], 1)
                mm.then_inc(act_turned, 1)
                turn_gates()
                pe.wait_ge(place_ready, turn + 1)
                gather(range(4))
                pe.wait_ge(act_t_ready, g + 1)
                for s in range(4):
                    pe.wait_ge(ring_full[DOWN + s], full)
                    for kk in range(2):
                        f = 2 * s + kk
                        mm = wide_product(0, act_t[:, f * P:(f + 1) * P], DOWN + s, kk, f == 0, f == KB - 1)
                    if s == 3:
                        mm.then_inc(down_done, 1)
                    elif last:
                        mm.then_inc(ring_free[DOWN + s], 1)
                pe.wait_ge(placeT_ready, g + 1)
                gather(range(4, KB), ring_free[DOWN + 3] if last else None)
                pe.wait_ge(y_ready, g + 1)
                for t in range(TB):
                    for half in range(2):
                        mm = nc.tensor.matmul(acc[:, 2 * t + half, :], place_gt[:, t * P:(t + 1) * P],
                                              y[:, half * 512:(half + 1) * 512],
                                              start=False, stop=True, skip_group_check=True)
                mm.then_inc(scattered, 1)

            def forget_gates(l):
                pe.wait_ge(small_full, l * SMALL + SMALL)
                for t in range(TB):
                    for k in range(KB):
                        mm = nc.tensor.matmul(acc[:, 1, t * N_FOX:(t + 1) * N_FOX], actT[:, k, t * P:(t + 1) * P],
                                              wf[:, k, :], start=(t == 0 and k == 0), stop=(k == KB - 1),
                                              skip_group_check=True)
                mm.then_inc(forget_z, 1)

            def project(l, c, t, ks, fulls):
                n = TB * c + t
                if ks[0] == 0:
                    if 2 <= n < 2 + TB * ROPE_CH:
                        pe.wait_ge(z_rope, l * TB * ROPE_CH + n - 1)
                    elif n >= 2:
                        pe.wait_ge(z_copied, l * TB * (N_CH - ROPE_CH) + n - 1 - TB * ROPE_CH)
                for k in ks:
                    if t == 0 and k % 4 == 0:
                        pe.wait_ge(ring_full[2 * c + k // 4], fulls[2 * c >= UP])
                    mm = nc.tensor.matmul(acc[:, 2 + t, :], actT[:, k, t * P:(t + 1) * P],
                                          ring[:, 2 * c + k // 4, (k % 4) * CH:(k % 4 + 1) * CH],
                                          start=(k == 0), stop=(k == KB - 1), skip_group_check=True)
                    if t == 1 and k == 3:
                        mm.then_inc(ring_free[2 * c], 1)
                    if t == 0 and k == 0 and c >= 1:
                        mm.then_inc(ring_free[2 * c - 1], 1)
                    if k == KB - 1:
                        mm.then_inc(z_done, 1)

            def sum_decay(l):
                pe.wait_ge(decay_ready, l + 1)
                nc.tensor.matmul(acc[:, 1, 0:N_FOX], tri0[:, 0:P], fg[:, 5, 0, :], start=True, stop=True,
                                 skip_group_check=True)
                nc.tensor.matmul(acc[:, 1, N_FOX:2 * N_FOX], ones, fg[:, 5, 0, :], start=False, stop=False,
                                 skip_group_check=True)
                nc.tensor.matmul(acc[:, 1, N_FOX:2 * N_FOX], tri0[:, 0:P], fg[:, 5, 1, :], start=False, stop=True,
                                 skip_group_check=True).then_inc(cum_done, 1)

            pe.wait_ge(ident_full, 16)
            with pe.Fori(0, DEPTH) as l:
                pe.wait_ge(plan_ready, l + 1)
                start = pe.value_load(start_i[0:1, bass.ds(l, 1)], min_val=0, max_val=MOST * DEPTH)
                for t in range(TB):
                    pe.wait_ge(h_ready, 4 * l + 1 + t)
                    turn_block(h, t)
                pe.wait_ge(actT_act, l * 10 + 4)
                gate_full = pe.snap(l * (16 * GATE_TURNS) + 16)
                fulls = (gate_full, pe.snap(l * (16 * TURNS) + 16))
                for c in range(4):
                    for t in range(TB):
                        project(l, c, t, range(KB), fulls)
                    if c == 0:
                        forget_gates(l)
                pe.wait_ge(const_full, 16 * CONST_LOADS)
                sum_decay(l)
                halves_of = [(c, t, ks) for c in (4, 5) for t in range(TB) for ks in (range(4), range(4, 8))]
                copied = l * TB * (N_CH - ROPE_CH)
                pe.wait_ge(z_rotated, (l + 1) * TB * ROPE_CH)
                pe.wait_ge(cum_read, l + 1)
                turn_qk(l, 0)
                for p in range(PAIRS + 1):
                    if p < 7:
                        project(l, *halves_of[p], fulls)
                    if p == 6:
                        turn_probs(l, 5)
                        weigh_values(l, 5)
                        project(l, *halves_of[7], fulls)
                        pe.wait_ge(z_copied, copied + 6)
                        turn_qk(l, 6, ring_free[2 * N_CH - 1])
                    if p < PAIRS:
                        scores(l, p)
                    if p + 1 < PAIRS and p != 5:
                        turn_qk(l, p + 1)
                    if p >= 1 and p != 6:
                        pe.wait_ge(z_copied, copied + (2 if p <= 4 else 4))
                        turn_probs(l, p - 1)
                        weigh_values(l, p - 1)
                seed(1)
                pe.wait_ge(mixed_done, (l + 1) * HEADS)
                seed(0)
                for t, normed in enumerate((normed0, normed1)):
                    pe.wait_ge(normed, l + 1)
                    turn_block(mixed, t)
                for t in range(TB):
                    pe.wait_ge(actT_dve, l * 2 + t + 1)
                    for k in range(KB):
                        if t == 0 and k % 2 == 0:
                            pe.wait_ge(ring_full[ODD + k // 2], gate_full)
                        if k == 4:
                            pe.wait_ge(actT_act, l * 10 + 4 + t + 1)
                        for half in range(2):
                            mm = nc.tensor.matmul(acc[:, 2 * t + half, :], actT[:, k, t * P:(t + 1) * P],
                                                  wout[:, k, half * 512:(half + 1) * 512],
                                                  start=False, stop=(k == KB - 1), skip_group_check=True)
                        if t == 1 and k in (1, 3, 5):
                            mm.then_inc(ring_free[ODD + k // 2], 1)
                    mm.then_inc(proj_done, 1)
                for t in range(TB):
                    pe.wait_ge(h_ready, 4 * l + 3 + t)
                    turn_block(h, t, ring_free[ODD + 3] if t == 0 else None)
                for t in range(TB):
                    pe.wait_ge(actT_act, l * 10 + 8 + 2 * t)
                    for k in range(KB):
                        mm = nc.tensor.matmul(lo[:, 0, t * NEXP:(t + 1) * NEXP], actT[:, k, t * P:(t + 1) * P],
                                              wr[:, k, :], start=(t == 0 and k == 0), stop=(k == KB - 1),
                                              skip_group_check=True)
                mm.then_inc(logits_done, 1)
                seed(0)
                seed(1)
                pe.wait_ge(sel_ready, l + 1)
                nc.tensor.matmul(lo[:, 1, 0:NEXP], tri0[:, 0:P], sel[:, 0, :], start=True, stop=True,
                                 skip_group_check=True)
                for at, mats in ((NEXP, (ones, tri0[:, 0:P])), (2 * NEXP, (ones, ones))):
                    for t in range(TB):
                        mm = nc.tensor.matmul(lo[:, 1, at:at + NEXP], mats[t], sel[:, t, :], start=False,
                                              stop=(t == 1), skip_group_check=True)
                mm.then_inc(ranks_done, 1)
                turn0 = pe.snap(start + l + 1)
                pe.wait_ge(place_ready, turn0)
                gather(range(KB))
                pe.wait_ge(plan_ready, l + 2)
                n = pe.value_load(n_i[0:1, bass.ds(l, 1)], min_val=NEXP, max_val=MOST)
                with pe.Fori(0, n) as j:
                    g = pe.snap(start + j)
                    turn = pe.snap(turn0 + j)
                    expert = pe.value_load(expert_i[0:1, bass.ds(l * ITEMS + j, 1)], min_val=0, max_val=NEXP - 1)
                    kind = pe.value_load(kind_i[0:1, bass.ds(l * ITEMS + j, 1)], min_val=0, max_val=2)
                    odd = pe.value_load(odd_i[0:1, bass.ds(expert, 1)], min_val=0, max_val=1)
                    full = pe.snap(l * (16 * TURNS) + expert * 16 + 32)
                    even_full = pe.snap(l * (16 * GATE_TURNS) + expert * 8 + 32)
                    odd_full = pe.snap(l * (16 * GATE_TURNS) + expert * 8 + 24)
                    pe.wait_ge(xg_ready, turn)
                    with pe.If(kind < 1):
                        with pe.If(odd < 1):
                            narrow_gate(EVEN, even_full, full)
                        with pe.Else():
                            narrow_gate(ODD, odd_full, full)
                        narrow_item(full, g, turn)
                    with pe.Else():
                        last = pe.value_load(last_i[0:1, bass.ds(l * ITEMS + j, 1)], min_val=0, max_val=1)
                        with pe.If(last > 0):
                            with pe.If(odd < 1):
                                wide_gate(True, EVEN, even_full, full)
                            with pe.Else():
                                wide_gate(True, ODD, odd_full, full)
                            wide_item(True, full, g, turn)
                        with pe.Else():
                            with pe.If(odd < 1):
                                wide_gate(False, EVEN, even_full, full)
                            with pe.Else():
                                wide_gate(False, ODD, odd_full, full)
                            wide_item(False, full, g, turn)

        @block.scalar
        def _(a):
            def root(out_ap, in_ap):
                return nc.scalar.activation(out_ap, in_ap, ACT.Sqrt)

            def roots(l, which):
                for t in range(TB):
                    a.wait_ge(var_ready, 4 * l + 2 * which + t + 1)
                    root(lnt[:, 1, t:t + 1], lnt[:, 0, t:t + 1]).then_inc(ln_root, 1)

            def copy_turned(l, use, banks):
                for b in banks:
                    a.wait_ge(turned, 12 * l + 4 * use + b + 1)
                    t, ks = b // 2, slice(4 * (b % 2), 4 * (b % 2) + 4)
                    nc.scalar.copy(actT[:, ks, t * P:(t + 1) * P], lo[:, b, :].rearrange("p (k s) -> p k s", k=4)
                                   ).then_inc(actT_act, 1)

            def copy_z(l, n):
                a.wait_ge(z_done, 12 * l + n + 1)
                c, t = n // TB, n % TB
                nc.scalar.copy(z[:, t, c * CH:(c + 1) * CH], acc[:, 2 + t, :]).then_inc(z_copied, 1)

            def copy_qk(l, p):
                a.wait_ge(qkT_done, l * PAIRS + p + 1)
                nc.scalar.copy(qkT[:, p % 2].rearrange("p a b -> p (a b)"), acc[:, 0, :]).then_inc(qkT_ready, 1)

            def exponentials(l, p):
                for i in range(2):
                    hd = 2 * p + i
                    a.wait_ge(masked_ready, l * HEADS + hd + 1)
                    if hd >= 4:
                        a.wait_ge(probsT_done, l * HEADS + hd - 3)
                    nc.scalar.activation(probs[:, hd % 4, 0:P], masked[:, i, 0:P], ACT.Exp,
                                         bias=neg_max[:, hd % 4, 0:1], scale=1 / INV_SCALE,
                                         accum_out=row_sum[:, hd % 4, 0:1])
                    nc.scalar.activation(probs[:, hd % 4, P:SKEYS], masked[:, i, P:SKEYS], ACT.Exp,
                                         bias=neg_max[:, hd % 4, 1:2], scale=1 / INV_SCALE,
                                         accum_out=row_sum[:, hd % 4, 1:2]).then_inc(exp_done, 1)

            def divide(l, p):
                a.wait_ge(pv_done, l * HEADS + 2 * p + 2)
                a.wait_ge(inv_ready, l * HEADS + 2 * p + 2)
                for i in range(2):
                    hd = 2 * p + i
                    for t in range(TB):
                        at = i * 2 * HD + t * HD
                        op = nc.scalar.mul(mixed[:, t, hd * HD:(hd + 1) * HD], acc[:, 1, at:at + HD],
                                           row_inv[:, i, t:t + 1])
                    op.then_inc(mixed_done, 1)

            def sum_squares(l, gi):
                c0, c1 = ((0, D_DIL), (D_DIL, D))[gi]
                for t in range(TB):
                    nc.scalar.activation(squares[:, 0:c1 - c0], mixed[:, t, c0:c1],
                                         ACT.Square, accum_out=ssq[:, t, gi:gi + 1]).then_inc(ssq_done, 1)
                    a.wait_ge(ssq_done, 4 * l + 2 * gi + t + 1)

            with a.Fori(0, DEPTH) as l:
                a.wait_ge(plan_ready, l + 1)
                start = a.value_load(start_i[0:1, bass.ds(l, 1)], min_val=0, max_val=MOST * DEPTH)
                copy_turned(l, 0, range(4))
                a.wait_ge(forget_arg, l + 1)
                nc.scalar.activation(fg[:, 3], fg[:, 2], ACT.Exp).then_inc(forget_log, 1)
                a.wait_ge(forget_log, 2 * l + 1)
                nc.scalar.activation(fg[:, 4], fg[:, 3], ACT.Ln, bias=1.0).then_inc(forget_log, 1)
                copy_z(l, 6)
                copy_z(l, 7)
                copy_qk(l, 0)
                for p in range(PAIRS + 1):
                    if p in (1, 3, 5):
                        copy_z(l, 8 + p // 2)
                    if p == 6:
                        divide(l, 5)
                        copy_z(l, 11)
                        copy_qk(l, 6)
                    if p + 1 < PAIRS and p != 5:
                        copy_qk(l, p + 1)
                    if p < PAIRS:
                        exponentials(l, p)
                    if p >= 1 and p != 6:
                        divide(l, p - 1)
                    if p == 7:
                        a.wait_ge(mixed_done, l * HEADS + N_DIL)
                        sum_squares(l, 0)
                a.wait_ge(mixed_done, (l + 1) * HEADS)
                sum_squares(l, 1)
                a.wait_ge(ms_ready, l + 1)
                root(rms[:, 1], rms[:, 0]).then_inc(rms_root, 1)
                a.wait_ge(rms_ready, l + 1)
                nc.scalar.mul(mixed[:, 1, 0:D_DIL], mixed[:, 1, 0:D_DIL], rms[:, 2, 1, 0:1])
                nc.scalar.mul(mixed[:, 1, D_DIL:D], mixed[:, 1, D_DIL:D], rms[:, 2, 1, 1:2]).then_inc(normed1, 1)
                for t in range(TB):
                    a.wait_ge(turned, 12 * l + 4 + 2 * t + 2)
                    for i in range(4):
                        op = nc.scalar.mul(actT[:, 4 + i, t * P:(t + 1) * P], lo[:, 2 * t + 1, i * P:(i + 1) * P],
                                           gmix[:, 4 + i:5 + i])
                    op.then_inc(actT_act, 1)
                roots(l, 0)
                copy_turned(l, 2, range(4))
                a.wait_ge(shifted, l + 1)
                nc.scalar.activation(rt[:, 1], rt[:, 0], ACT.Exp).then_inc(router_exp, 1)
                a.wait_ge(gathered, a.snap(2 * start + 2 * l + 2))
                for b in range(2):
                    op = nc.scalar.copy(xg[:, 4 * b:4 * b + 4, :], lo[:, 2 + b, :].rearrange("p (k s) -> p k s", k=4))
                op.then_inc(xg_ready, 1)
                a.wait_ge(plan_ready, l + 2)
                a.sem_inc(passed, 1)
                n = a.value_load(n_i[0:1, bass.ds(l, 1)], min_val=NEXP, max_val=MOST)
                with a.Fori(0, n) as j:
                    g = a.snap(start + j)
                    kind = a.value_load(kind_i[0:1, bass.ds(l * ITEMS + j, 1)], min_val=0, max_val=2)
                    with a.If(kind < 1):
                        a.wait_ge(gate_done, g + 1)
                        nc.scalar.activation(silu[:, 0:512], lo[:, 0, :], ACT.Silu).then_inc(silu_done, 1)
                        a.wait_ge(act_turned, g + 1)
                        nc.scalar.copy(act_t[:, 0:512], lo[:, 1, :]).then_inc(act_t_ready, 1)
                    with a.Else():
                        a.wait_ge(gate_done, g + 1)
                        for half in range(2):
                            op = nc.scalar.activation(silu[:, half * 512:(half + 1) * 512], lo[:, half, :], ACT.Silu)
                        op.then_inc(silu_done, 1)
                        a.wait_ge(act_turned, g + 1)
                        for half in range(2):
                            op = nc.scalar.copy(act_t[:, half * 512:(half + 1) * 512], lo[:, half, :])
                        op.then_inc(act_t_ready, 1)
                roots(l, 1)

        @block.vector
        def _(v):
            DVE_STEPS = 77
            steps = [0]
            base = [0]

            def step(ins):
                steps[0] += 1
                ins.then_inc(dve_step, 1)
                v.wait_ge(dve_step, base[0] + steps[0])

            def layer_norm(l, which, t):
                for half in range(2):
                    op = nc.vector.bn_stats(stats[:, t, half, :], acc[:, 2 * t + half, :])
                step(op)
                v.sem_inc(passed, 1)
                step(nc.vector.bn_aggr(mv[:, t, :], stats[:, t].rearrange("p a b -> p (a b)")))
                nc.vector.tensor_scalar(lnt[:, 0, t:t + 1], mv[:, t, 1:2], LN_EPS, None, ALU.add).then_inc(var_ready, 1)
                v.wait_ge(ln_full, 64 * l + 32 * (which + 1))
                nc.vector.scalar_tensor_tensor(out=h[:, t, :], in0=acc_tok[:, t, :], scalar=mv[:, t, 0:1],
                                               in1=ln_gb[:, 0, :], op0=ALU.subtract, op1=ALU.mult)
                v.wait_ge(ln_root, 4 * l + 2 * which + t + 1)
                step(nc.vector.reciprocal(lnt[:, 2, t:t + 1], lnt[:, 1, t:t + 1]))
                nc.vector.scalar_tensor_tensor(out=h[:, t, :], in0=h[:, t, :], scalar=lnt[:, 2, t:t + 1],
                                               in1=ln_gb[:, 1, :], op0=ALU.mult, op1=ALU.add).then_inc(h_ready, 1)

            def mask(l, p):
                for i in range(2):
                    hd = 2 * p + i
                    v.wait_ge(scores_done, l * HEADS + hd + 1)
                    if hd >= 2:
                        v.wait_ge(exp_done, l * HEADS + hd - 1)
                    if hd < N_DIL:
                        op = nc.vector.tensor_tensor(masked[:, i, :], lo[:, i, 0:SKEYS],
                                                     cst[:, C_MDIL:C_MDIL + SKEYS], ALU.add)
                    else:
                        f = hd - N_DIL
                        for t, (c0, c1) in enumerate(((0, P), (P, SKEYS))):
                            op = nc.vector.scalar_tensor_tensor(
                                out=masked[:, i, c0:c1], in0=lo[:, i, c0:c1], scalar=fg[:, 0, t, f:f + 1],
                                in1=cst[:, C_MFOX + c0:C_MFOX + c1], op0=ALU.subtract, op1=ALU.add)
                    step(op)
                    nc.vector.tensor_reduce(row_max[:, i, 0:1], masked[:, i, 0:P], AX.X, ALU.max)
                    step(nc.vector.tensor_reduce(row_max[:, i, 1:2], masked[:, i, P:SKEYS], AX.X, ALU.max))
                    nc.vector.tensor_scalar(neg_max[:, hd % 4, :], row_max[:, i, :], -1 / INV_SCALE, None,
                                            ALU.mult).then_inc(masked_ready, 1)

            def copy_probs(l, p):
                for i in range(2):
                    hd = 2 * p + i
                    v.wait_ge(probsT_done, l * HEADS + hd + 1)
                    nc.vector.tensor_copy(probsT[:, i, :], lo[:, 2 + i, 0:SKEYS]).then_inc(probsT_ready, 1)
                    if hd >= 2:
                        v.wait_ge(mixed_done, l * HEADS + hd - 1)
                    nc.vector.reciprocal(row_inv[:, i, :], row_sum[:, hd % 4, :]).then_inc(inv_ready, 1)

            def ranks(dst, src, n):
                vals = src.rearrange("p (n i) -> p n i", i=4)
                vj = vals.unsqueeze(2).to_broadcast([P, n, 4, 4])
                vi = vals.unsqueeze(3).to_broadcast([P, n, 4, 4])
                ca, cb = (cmp[:, i, 0:16 * n] for i in range(2))
                nc.vector.tensor_tensor(ca.rearrange("p (n i j) -> p n i j", i=4, j=4), vj, vi, ALU.is_gt)
                step(nc.vector.tensor_tensor(cb.rearrange("p (n i j) -> p n i j", i=4, j=4), vj, vi, ALU.is_ge))
                nc.vector.tensor_tensor(ca, ca, cst[:, C_UP:C_UP + 16 * n], ALU.mult)
                step(nc.vector.tensor_tensor(cb, cb, cst[:, C_LO:C_LO + 16 * n], ALU.mult))
                step(nc.vector.tensor_tensor(ca, ca, cb, ALU.add))
                step(nc.vector.tensor_reduce(dst, ca.rearrange("p (n j) -> p n j", j=4), AX.X, ALU.add))

            def place_tokens(expert, kind):
                for t in range(TB):
                    op = nc.vector.tensor_scalar(place_t[:, t], places[:, bass.ds(kind * P, P)],
                                                 rank_tab[:, t, bass.ds(expert, 1)], None, ALU.is_equal)
                op.then_inc(place_ready, 1)

            def place_gates(expert, kind):
                for t in range(TB):
                    nc.vector.tensor_scalar(place_tg[:, t], places[:, bass.ds(kind * P, P)],
                                            rank_tab[:, t, bass.ds(expert, 1)], gate_tab[:, t, bass.ds(expert, 1)],
                                            ALU.is_equal, ALU.mult)

            def copy_gathered(turn, half):
                v.wait_ge(gathered, turn * 2 + half + 1)
                op = nc.vector.tensor_copy(xg[:, 4 * half:4 * half + 4, :],
                                           lo[:, 2 + half, :].rearrange("p (k s) -> p k s", k=4))
                if half == 1:
                    op.then_inc(xg_ready, 1)

            def copy_gates(g):
                v.wait_ge(placeT_done, g + 1)
                nc.vector.tensor_copy(place_gt, lo[:, 3, 0:SEQ]).then_inc(placeT_ready, 1)

            nc.vector.memset(startf[:], 0.0)
            nc.vector.memset(wide[:], 0.0)
            nc.vector.memset(start_i[:], 0)
            nc.vector.memset(itab[:], 0.0).then_inc(plan_ready, 1)
            v.wait_ge(x_full, 16)
            nc.vector.memset(nsub[:, 0], 0.0).then_inc(h_ready, 1)
            nc.vector.memset(nsub[:, 1], 0.0).then_inc(h_ready, 1)
            with v.Fori(0, DEPTH) as l:
                base[0] = v.snap(l * DVE_STEPS)
                v.wait_ge(plan_ready, l + 1)
                start = v.value_load(start_i[0:1, bass.ds(l, 1)], min_val=0, max_val=MOST * DEPTH)
                for n in range(TB * ROPE_CH):
                    c, t = n // TB, n % TB
                    src = acc[:, 2 + t, :].rearrange("p (h two i) -> p h two i", two=2, i=32)
                    dst = z[:, t, c * CH:(c + 1) * CH].rearrange("p (h two i) -> p h two i", two=2, i=32)
                    cos, sin = (cst[:, C_COS + t * 64 + i * 32:C_COS + t * 64 + (i + 1) * 32].unsqueeze(1)
                                .to_broadcast([P, 8, 32]) for i in range(2))
                    t2sin = cmp[:, 0, :].rearrange("p (h i) -> p h i", i=32)
                    t1sin = cmp[:, 1, :].rearrange("p (h i) -> p h i", i=32)
                    if n == 0:
                        v.wait_ge(const_full, 16 * CONST_LOADS)
                    v.wait_ge(z_done, 12 * l + n + 1)
                    nc.vector.tensor_tensor(dst[:, :, 0], src[:, :, 0], cos, ALU.mult)
                    nc.vector.tensor_tensor(t2sin, src[:, :, 1], sin, ALU.mult)
                    nc.vector.tensor_tensor(dst[:, :, 1], src[:, :, 1], cos, ALU.mult)
                    ins = nc.vector.tensor_tensor(t1sin, src[:, :, 0], sin, ALU.mult)
                    ins.then_inc(z_rope, 1)
                    v.wait_ge(z_rope, l * TB * ROPE_CH + n + 1)
                    nc.vector.tensor_tensor(dst[:, :, 0], dst[:, :, 0], t2sin, ALU.subtract)
                    nc.vector.tensor_tensor(dst[:, :, 1], dst[:, :, 1], t1sin, ALU.add).then_inc(z_rotated, 1)
                    v.wait_ge(z_rotated, l * TB * ROPE_CH + n + 1)
                    if n == 1:
                        v.wait_ge(forget_z, l + 1)
                        step(nc.vector.tensor_tensor(fg[:, 0],
                                                     acc[:, 1, 0:TB * N_FOX].rearrange("p (t n) -> p t n", t=TB),
                                                     bf[:].to_broadcast([P, TB, N_FOX]), ALU.add))
                        nc.vector.tensor_scalar(fg[:, 1], fg[:, 0], -1.0, 0.0, ALU.mult, ALU.max)
                        nc.vector.scalar_tensor_tensor(out=fg[:, 2], in0=fg[:, 0], scalar=-1.0, in1=fg[:, 0],
                                                       op0=ALU.mult, op1=ALU.min).then_inc(forget_arg, 1)
                v.wait_ge(forget_log, 2 * l + 2)
                step(nc.vector.tensor_tensor(fg[:, 6], fg[:, 1], fg[:, 4], ALU.add))
                step(nc.vector.tensor_scalar(fg[:, 5], fg[:, 6], INV_SCALE, None, ALU.mult))
                for t in range(TB):
                    for f in range(N_FOX):
                        op = nc.vector.tensor_scalar(decay[:, t, f, :], ones, fg[:, 5, t, f:f + 1], None, ALU.mult)
                op.then_inc(decay_ready, 1)
                v.wait_ge(cum_done, l + 1)
                nc.vector.tensor_copy(fg[:, 0].rearrange("p t n -> p (t n)"), acc[:, 1, 0:TB * N_FOX]
                                      ).then_inc(cum_read, 1)
                for p in range(PAIRS + 1):
                    if p == 6:
                        copy_probs(l, 5)
                    if p < PAIRS:
                        mask(l, p)
                    if p >= 1 and p != 6:
                        copy_probs(l, p - 1)
                v.wait_ge(ssq_done, 4 * l + 4)
                nc.vector.tensor_scalar(rms[:, 0, :, 0], ssq[:, :, 0], 1.0 / D_DIL, RMS_EPS, ALU.mult, ALU.add)
                nc.vector.tensor_scalar(rms[:, 0, :, 1], ssq[:, :, 1], 1.0 / D_FOX, RMS_EPS, ALU.mult, ALU.add
                                        ).then_inc(ms_ready, 1)
                v.wait_ge(rms_root, l + 1)
                nc.vector.reciprocal(rms[:, 2], rms[:, 1]).then_inc(rms_ready, 1)
                v.wait_ge(rms_ready, l + 1)
                nc.vector.tensor_scalar(mixed[:, 0, 0:D_DIL], mixed[:, 0, 0:D_DIL], rms[:, 2, 0, 0:1], None, ALU.mult)
                nc.vector.tensor_scalar(mixed[:, 0, D_DIL:D], mixed[:, 0, D_DIL:D], rms[:, 2, 0, 1:2], None,
                                        ALU.mult).then_inc(normed0, 1)
                for t in range(TB):
                    v.wait_ge(turned, 12 * l + 4 + 2 * t + 1)
                    nc.vector.tensor_tensor(actT[:, 0:4, t * P:(t + 1) * P],
                                            lo[:, 2 * t, :].rearrange("p (k s) -> p k s", k=4),
                                            gmix[:, 0:4].unsqueeze(2).to_broadcast([P, 4, P]), ALU.mult
                                            ).then_inc(actT_dve, 1)
                for t in range(TB):
                    v.wait_ge(proj_done, 2 * l + t + 2)
                    layer_norm(l, 0, t)
                v.wait_ge(logits_done, l + 1)
                step(nc.vector.tensor_tensor(rt[:, 2], lo[:, 0, 0:TB * NEXP].rearrange("p (t e) -> p t e", t=TB),
                                             br[:].to_broadcast([P, TB, NEXP]), ALU.add))
                step(nc.vector.tensor_reduce(r2[:, 0], rt[:, 2], AX.X, ALU.max))
                nc.vector.tensor_tensor(rt[:, 0], rt[:, 2], r2[:, 0].unsqueeze(2).to_broadcast([P, TB, NEXP]),
                                        ALU.subtract).then_inc(shifted, 1)
                v.wait_ge(router_exp, l + 1)
                step(nc.vector.tensor_reduce(r2[:, 1], rt[:, 1], AX.X, ALU.add))
                step(nc.vector.reciprocal(r2[:, 2], r2[:, 1]))
                step(nc.vector.tensor_tensor(rt[:, 2], rt[:, 1], r2[:, 2].unsqueeze(2).to_broadcast([P, TB, NEXP]),
                                             ALU.mult))
                probs16 = rt[:, 2].rearrange("p t e -> p (t e)")
                in_grp = rt[:, 3].rearrange("p t e -> p (t e)")
                ranks(in_grp, probs16, 8)
                best = rt[:, 4].rearrange("p t e -> p (t e)")
                step(nc.vector.scalar_tensor_tensor(out=best, in0=in_grp, scalar=1.5, in1=probs16, op0=ALU.is_lt,
                                                    op1=ALU.mult))
                step(nc.vector.tensor_reduce(r8[:, 0], best.rearrange("p (g i) -> p g i", i=4), AX.X, ALU.add))
                ranks(r8[:, 1], r8[:, 0], 2)
                step(nc.vector.tensor_scalar(r8[:, 2], r8[:, 1], 0.5, None, ALU.is_lt))
                chosen = r8[:, 2].unsqueeze(2).to_broadcast([P, 8, 4])
                nc.vector.scalar_tensor_tensor(out=sel[:].rearrange("p t (g i) -> p (t g) i", i=4),
                                               in0=in_grp.rearrange("p (g i) -> p g i", i=4), scalar=1.5, in1=chosen,
                                               op0=ALU.is_lt, op1=ALU.mult).then_inc(sel_ready, 1)
                step(nc.vector.tensor_tensor(rt[:, 5].rearrange("p t (g i) -> p (t g) i", i=4),
                                             best.rearrange("p (g i) -> p g i", i=4), chosen, ALU.mult))
                step(nc.vector.tensor_reduce(r2[:, 3], rt[:, 5], AX.X, ALU.add))
                step(nc.vector.reciprocal(r2[:, 4], r2[:, 3]))
                nc.vector.tensor_tensor(gate_tab[:], rt[:, 5],
                                        r2[:, 4].unsqueeze(2).to_broadcast([P, TB, NEXP]), ALU.mult)
                v.wait_ge(ranks_done, l + 1)
                nc.vector.tensor_scalar(wide_shift[:], lo[:, 1, 2 * NEXP:2 * NEXP + 1], W + 0.5, float(W), ALU.is_gt,
                                        ALU.mult)
                step(nc.vector.tensor_tensor(rank_tab[:],
                                             lo[:, 1, 0:TB * NEXP].rearrange("p (t e) -> p t e", t=TB), sel[:],
                                             ALU.mult))
                turn0 = v.snap(start + l + 1)
                for t in range(TB):
                    nc.vector.tensor_scalar(place_t[:, t, 0:W], iota[:, 0:W], rank_tab[:, t, 0:1], None, ALU.is_equal)
                for t in range(TB):
                    op = nc.vector.tensor_scalar(place_t[:, t, W:P], iota[:, 0:W], wide_shift[:],
                                                 rank_tab[:, t, 0:1], ALU.add, ALU.is_equal)
                op.then_inc(place_ready, 1)
                count = lo[:, 1, 2 * NEXP:3 * NEXP]
                nc.vector.tensor_scalar(wide[:, 0:NEXP], count, W + 0.5, None, ALU.is_gt)
                step(nc.vector.tensor_scalar(nsub[:, 0], count, P + 0.5, 1.0, ALU.is_gt, ALU.add))
                step(nc.vector.tensor_tensor(kind_step[:, 0], wide[:, 1:NEXP + 1], wide[:, 0:NEXP], ALU.subtract))
                nc.vector.tensor_tensor(kind_step[:, 1], kind_step[:, 0], nsub[:, 0], ALU.subtract)
                upto = pscratch[:, 0:NEXP * NEXP].rearrange("p (e f) -> p e f", e=NEXP)
                step(nc.vector.tensor_tensor(upto, cst[:, C_L16:C_L16 + 256].rearrange("p (e f) -> p e f", e=NEXP),
                                             nsub[:, 0].unsqueeze(1).to_broadcast([P, NEXP, NEXP]), ALU.mult))
                step(nc.vector.tensor_reduce(nsub[:, 1], upto, AX.X, ALU.add))
                ended, ends = (pscratch[:, c:c + ITEMS * NEXP].rearrange("p (i e) -> p i e", i=ITEMS)
                               for c in (256, 768))
                cum = nsub[:, 1].unsqueeze(1).to_broadcast([P, ITEMS, NEXP])
                count_i = iota[:, 0:ITEMS].unsqueeze(2).to_broadcast([P, ITEMS, NEXP])
                nc.vector.tensor_tensor(ends, cum, count_i, ALU.is_equal)
                step(nc.vector.tensor_tensor(ended, cum, count_i, ALU.is_lt))
                nc.vector.tensor_reduce(itab[:, 2], ends, AX.X, ALU.add)
                step(nc.vector.tensor_reduce(itab[:, 0], ended, AX.X, ALU.add))
                step(nc.vector.tensor_tensor(ended, ended, kind_step[:, 1].unsqueeze(1).to_broadcast([P, ITEMS, NEXP]),
                                             ALU.mult))
                step(nc.vector.tensor_reduce(itab[:, 1], ended, AX.X, ALU.add))
                step(nc.vector.scalar_tensor_tensor(out=itab[:, 3], in0=itab[:, 1], scalar=wide[:, 0:1],
                                                    in1=iota[:, 0:ITEMS], op0=ALU.add, op1=ALU.add))
                own = l * ITEMS
                nc.vector.tensor_copy(odd_i[:], cst[:, C_ODD:C_END])
                nc.vector.tensor_scalar(expert_i[:, bass.ds(own, ITEMS)], itab[:, 0], NEXP - 1.0, None, ALU.min)
                nc.vector.tensor_scalar(kind_i[:, bass.ds(own, ITEMS)], itab[:, 3], -1.0, 0.0, ALU.add, ALU.max)
                nc.vector.tensor_copy(last_i[:, bass.ds(own, ITEMS)], itab[:, 2])
                nc.vector.tensor_copy(n_i[:, bass.ds(l, 1)], nsub[:, 1, NEXP - 1:NEXP])
                step(nc.vector.tensor_tensor(startf[:, bass.ds(l + 1, 1)], startf[:, bass.ds(l, 1)],
                                             nsub[:, 1, NEXP - 1:NEXP], ALU.add))
                nc.vector.tensor_copy(start_i[:, bass.ds(l + 1, 1)], startf[:, bass.ds(l + 1, 1)]
                                      ).then_inc(plan_ready, 1)
                v.wait_ge(plan_ready, l + 2)
                v.wait_ge(gathered, turn0 * 2)
                v.sem_inc(passed, 1)
                n = v.value_load(n_i[0:1, bass.ds(l, 1)], min_val=NEXP, max_val=MOST)
                with v.Fori(0, n) as j:
                    g = v.snap(start + j)
                    turn = v.snap(turn0 + j)
                    at = v.snap(l * ITEMS + j)
                    kind = v.value_load(kind_i[0:1, bass.ds(at, 1)], min_val=0, max_val=2)
                    place_gates(v.value_load(expert_i[0:1, bass.ds(at, 1)], min_val=0, max_val=NEXP - 1), kind)
                    place_tokens(v.value_load(expert_i[0:1, bass.ds(at + 1, 1)], min_val=0, max_val=NEXP - 1),
                                 v.value_load(kind_i[0:1, bass.ds(at + 1, 1)], min_val=0, max_val=2))
                    v.wait_ge(up_done, g + 1)
                    v.wait_ge(silu_done, g + 1)
                    v.sem_inc(passed, 1)
                    with v.If(kind < 1):
                        nc.vector.tensor_tensor(act[:, 0:512], lo[:, 1, :], silu[:, 0:512], ALU.mult
                                                ).then_inc(act_ready, 1)
                        copy_gates(g)
                        copy_gathered(turn, 0)
                        v.wait_ge(down_done, g + 1)
                        nc.vector.tensor_copy(y[:, 0:512], lo[:, 0, :]).then_inc(y_ready, 1)
                        copy_gathered(turn, 1)
                    with v.Else():
                        for half in range(2):
                            at = slice(half * 512, (half + 1) * 512)
                            op = nc.vector.tensor_tensor(act[:, at], lo[:, 2 + half, :], silu[:, at], ALU.mult)
                        op.then_inc(act_ready, 1)
                        copy_gates(g)
                        copy_gathered(turn, 0)
                        v.wait_ge(down_done, g + 1)
                        for half in range(2):
                            op = nc.vector.tensor_copy(y[:, half * 512:(half + 1) * 512], lo[:, half, :])
                        op.then_inc(y_ready, 1)
                        copy_gathered(turn, 1)
                v.wait_ge(scattered, start + n)
                for t in range(TB):
                    layer_norm(l, 1, t)
            assert steps[0] == DVE_STEPS, steps[0]


_INS = ['x', 'w_in', 'b_forget', 'g_dil', 'g_fox', 'w_out', 'ln1_g', 'ln1_b', 'w_router', 'b_router',
        'w_gate', 'w_up', 'w_down', 'ln2_g', 'ln2_b']


def kernel(**inputs):
    import numpy as _np
    import concourse.bacc as _bacc
    from concourse import mybir as _mybir
    from concourse.bass_utils import run_bass_kernel_spmd as _run

    nc = _bacc.Bacc("TRN2", target_bir_lowering=False, num_devices=1, dynamic_dma_scratch_size=8192)
    arrays, args = {}, []
    for name in _INS + ['consts']:
        a = constants() if name == 'consts' else _np.ascontiguousarray(inputs[name])
        arrays[f"in_{name}_dram"] = a
        args.append(nc.dram_tensor(f"in_{name}_dram", a.shape, _mybir.dt.from_np(a.dtype), kind="ExternalInput").ap())
    args.append(nc.dram_tensor("out_dram", (1, SEQ, D), F32, kind="ExternalOutput").ap())
    build(nc, *args)
    r = _run(nc, [arrays], core_ids=[0])
    return r.results[0]["out_dram"]
```
